# Optimizing a Trainium2 kernel written in Bass

```python
import jax, jax.numpy as jnp
from jax import lax
import numpy as np

D_MODEL = 1024
BATCH = 1
SEQ = 256
DEPTH = 2

N_META = 16
D_MIX = D_MODEL
POOL_WIDTH = D_MIX // 4
POOL_WINDOWS = (2, 4, 8, 16)
POOL_GROUP = POOL_WIDTH // len(POOL_WINDOWS)
CONV_WIDTH = D_MIX // 4
CONV_K = 3
GLA_WIDTH = D_MIX // 2
GLA_HEADS = 4
GLA_DV = GLA_WIDTH // GLA_HEADS
GLA_DK = GLA_DV // 2
GLA_KW = GLA_HEADS * GLA_DK
GLA_GATE_RANK = 16
GLA_TAU = 16.0
GLA_CHUNK = 64
D_FF = 2816
FFN_RESID = 0.5
EPS = 1e-6
PROJ_SIZES = (POOL_WIDTH, CONV_WIDTH, CONV_WIDTH, CONV_WIDTH, GLA_KW, GLA_KW, GLA_WIDTH, GLA_GATE_RANK, GLA_WIDTH)
D_PROJ = sum(PROJ_SIZES)

kernel_name = 'hymba_pool_conv_gla_macaron_block'

def rms_norm(x, g):
    xf = x.astype(jnp.float32)
    y = xf * lax.rsqrt(jnp.mean(xf * xf, axis=-1, keepdims=True) + EPS)
    return (y * g.astype(jnp.float32)).astype(x.dtype)

def swiglu(h, w_gate, w_up, w_down):
    return (jax.nn.silu(h @ w_gate) * (h @ w_up)) @ w_down

def pool_mixer(p, w_group, scale):
    B, L, _ = p.shape
    pg = p.reshape(B, L, len(POOL_WINDOWS), POOL_GROUP).astype(jnp.float32)
    csum = jnp.cumsum(pg, axis=1)
    pos = jnp.arange(1, L + 1, dtype=jnp.float32)
    outs = []
    for i, w in enumerate(POOL_WINDOWS):
        ci = csum[:, :, i]
        prev = jnp.pad(ci, ((0, 0), (w, 0), (0, 0)))[:, :L]
        cnt = jnp.minimum(pos, float(w))[None, :, None]
        outs.append((ci - prev) / cnt - pg[:, :, i])
    m = jnp.stack(outs, axis=2).astype(p.dtype)
    y = jnp.einsum('blgc,gcd->blgd', m, w_group)
    return y.reshape(B, L, POOL_WIDTH) * scale

def conv_mixer(gate_b, gate_c, u, w_conv):
    z = gate_c * u
    y = lax.conv_general_dilated(
        z, w_conv[:, None, :].astype(z.dtype), window_strides=(1,),
        padding=[(CONV_K - 1, 0)], dimension_numbers=('NWC', 'WIO', 'NWC'),
        feature_group_count=CONV_WIDTH)
    return gate_b * y

def gla_mixer(q, k, v, g_low, out_gate, w_g2, b_g2, norm_g):
    B, L, _ = q.shape
    out_dtype = q.dtype
    f32 = jnp.float32
    log_a = jax.nn.log_sigmoid((g_low @ w_g2 + b_g2).astype(f32)) / GLA_TAU
    pad_front = (-N_META) % GLA_CHUNK
    Lp = L + pad_front
    n_chunks = Lp // GLA_CHUNK

    def to_chunks(t, d):
        t = jnp.pad(t.astype(f32), ((0, 0), (pad_front, 0), (0, 0)))
        t = t.reshape(B, n_chunks, GLA_CHUNK, GLA_HEADS, d)
        return t.transpose(1, 0, 3, 2, 4)

    qc = to_chunks(q, GLA_DK) * (GLA_DK ** -0.5)
    kc = to_chunks(k, GLA_DK)
    vc = to_chunks(v, GLA_DV)
    gc = to_chunks(log_a, GLA_DK)
    causal = jnp.tril(jnp.ones((GLA_CHUNK, GLA_CHUNK), dtype=bool))

    def step(S, inp):
        qi, ki, vi, gi = inp
        b = jnp.cumsum(gi, axis=2)
        inter = jnp.einsum('bhtd,bhde->bhte', qi * jnp.exp(b), S)
        diff = b[:, :, :, None, :] - b[:, :, None, :, :]
        decay = jnp.exp(jnp.where(causal[:, :, None], diff, -jnp.inf))
        scores = jnp.einsum('bhtd,bhsd,bhtsd->bhts', qi, ki, decay)
        intra = jnp.einsum('bhts,bhse->bhte', scores, vi)
        b_last = b[:, :, -1:, :]
        S = S * jnp.exp(b_last[:, :, 0, :])[..., None] + jnp.einsum(
            'bhsd,bhse->bhde', ki * jnp.exp(b_last - b), vi)
        return S, inter + intra

    S0 = jnp.zeros((B, GLA_HEADS, GLA_DK, GLA_DV), f32)
    _, o = lax.scan(step, S0, (qc, kc, vc, gc))
    o = o.transpose(1, 0, 3, 2, 4).reshape(B, Lp, GLA_HEADS, GLA_DV)[:, pad_front:]
    o = o * lax.rsqrt(jnp.mean(o * o, axis=-1, keepdims=True) + EPS)
    o = o * norm_g.reshape(GLA_HEADS, GLA_DV).astype(f32)
    o = o.reshape(B, L, GLA_WIDTH) * jax.nn.silu(out_gate.astype(f32))
    return o.astype(out_dtype)

def setup_inputs(seed: int = 0) -> dict:
    key = jax.random.key(seed)
    ks = jax.random.split(key, 22)
    f32 = jnp.float32
    nrm = lambda k, shape, s: jax.random.normal(k, shape, f32) * s
    gain = lambda k, shape: 1.0 + 0.02 * jax.random.normal(k, shape, f32)
    return {
        'x': nrm(ks[0], (BATCH, SEQ, D_MODEL), 1.0),
        'meta': nrm(ks[1], (N_META, D_MODEL), 1.0),
        'ffn1_pre': gain(ks[2], (DEPTH, D_MODEL)),
        'ffn1_post': gain(ks[3], (DEPTH, D_MODEL)),
        'ffn1_wg': nrm(ks[4], (DEPTH, D_MODEL, D_FF), D_MODEL ** -0.5),
        'ffn1_wu': nrm(ks[5], (DEPTH, D_MODEL, D_FF), D_MODEL ** -0.5),
        'ffn1_wd': nrm(ks[6], (DEPTH, D_FF, D_MODEL), D_FF ** -0.5),
        'mix_pre': gain(ks[7], (DEPTH, D_MODEL)),
        'mix_post': gain(ks[8], (DEPTH, D_MODEL)),
        'w_in': nrm(ks[9], (DEPTH, D_MODEL, D_PROJ), D_MODEL ** -0.5),
        'pool_w': nrm(ks[10], (DEPTH, len(POOL_WINDOWS), POOL_GROUP, POOL_GROUP), POOL_GROUP ** -0.5),
        'pool_scale': gain(ks[11], (DEPTH, POOL_WIDTH)),
        'conv_w': nrm(ks[12], (DEPTH, CONV_K, CONV_WIDTH), CONV_K ** -0.5),
        'gla_w2': nrm(ks[13], (DEPTH, GLA_GATE_RANK, GLA_KW), GLA_GATE_RANK ** -0.5),
        'gla_b2': nrm(ks[14], (DEPTH, GLA_KW), 0.01),
        'gla_norm': gain(ks[15], (DEPTH, GLA_WIDTH)),
        'w_out': nrm(ks[16], (DEPTH, D_MIX, D_MODEL), D_MIX ** -0.5),
        'ffn2_pre': gain(ks[17], (DEPTH, D_MODEL)),
        'ffn2_post': gain(ks[18], (DEPTH, D_MODEL)),
        'ffn2_wg': nrm(ks[19], (DEPTH, D_MODEL, D_FF), D_MODEL ** -0.5),
        'ffn2_wu': nrm(ks[20], (DEPTH, D_MODEL, D_FF), D_MODEL ** -0.5),
        'ffn2_wd': nrm(ks[21], (DEPTH, D_FF, D_MODEL), D_FF ** -0.5),
    }

def reference(x, meta, ffn1_pre, ffn1_post, ffn1_wg, ffn1_wu, ffn1_wd,
              mix_pre, mix_post, w_in, pool_w, pool_scale, conv_w,
              gla_w2, gla_b2, gla_norm, w_out,
              ffn2_pre, ffn2_post, ffn2_wg, ffn2_wu, ffn2_wd):
    B = x.shape[0]
    h = jnp.concatenate(
        [jnp.broadcast_to(meta.astype(x.dtype)[None], (B, N_META, D_MODEL)), x], axis=1)
    split_idx = np.cumsum(PROJ_SIZES)[:-1].tolist()
    for l in range(DEPTH):
        f = swiglu(rms_norm(h, ffn1_pre[l]), ffn1_wg[l], ffn1_wu[l], ffn1_wd[l])
        h = h + FFN_RESID * rms_norm(f, ffn1_post[l])
        a = rms_norm(h, mix_pre[l])
        proj = a @ w_in[l]
        p_pool, c_b, c_c, c_u, g_q, g_k, g_v, g_low, g_out = jnp.split(proj, split_idx, axis=-1)
        y_pool = pool_mixer(p_pool, pool_w[l], pool_scale[l])
        y_conv = conv_mixer(c_b, c_c, c_u, conv_w[l])
        y_gla = gla_mixer(g_q, g_k, g_v, g_low, g_out, gla_w2[l], gla_b2[l], gla_norm[l])
        mix = jnp.concatenate([y_pool, y_conv, y_gla], axis=-1) @ w_out[l]
        h = h + rms_norm(mix, mix_post[l])
        f = swiglu(rms_norm(h, ffn2_pre[l]), ffn2_wg[l], ffn2_wu[l], ffn2_wd[l])
        h = h + FFN_RESID * rms_norm(f, ffn2_post[l])
    return h[:, N_META:]


_drawn_inputs = setup_inputs


def setup_inputs(seed=0):
    import zlib

    import numpy as np

    out = dict(_drawn_inputs(seed))
    spreads = {}
    factors = {'ffn1_post': 3.232,
     'mix_post': 2.691,
     'pool_scale': 12.181,
     'gla_b2': 8.0,
     'gla_norm': 13.593,
     'ffn2_pre': 4.072,
     'ffn2_post': 16.417}
    for name, (base, spread) in spreads.items():
        noise = np.random.default_rng([zlib.crc32(name.encode()), seed]).standard_normal(out[name].shape)
        drawn = base * np.exp(spread * noise) if base else spread * noise
        out[name] = __import__('jax').numpy.asarray(drawn.astype(out[name].dtype))
    for name, factor in factors.items():
        out[name] = (out[name] * factor).astype(out[name].dtype)
    return out
```

```python
from contextlib import ExitStack

import numpy as np
import concourse.bass as bass
from concourse import mybir

ALU = mybir.AluOpType
ACT = mybir.ActivationFunctionType
F32 = mybir.dt.float32
F32R = mybir.dt.float32r
I32 = mybir.dt.int32
U32 = mybir.dt.uint32

P = 128
NMETA = 16
D = 1024
KT = D // P
FF = 2816
FT = FF // P
GROUPS = FT // 2
HEADS = 4
EPS = 1e-6
RING = 4
UNIT = 2048
DOWN_K = (6, 6, 5, 5)
MAGIC = float(0x5F3759DF)
LOG_DECAY_MIN = -60.0
MIX_UNITS = 15
Q_QK, Q_V, Q_GOUT, Q_POOL_CB, Q_CC_CU = 1024, 1536, 2064, 0, 512
C_GLOW = 2048
POOL_WINDOWS = (2, 4, 8, 16)
BASE = 2
LEVELS = (4, 8, 16, 32, 64)
JOBS = 9


def shape_constants(T):
    c = np.zeros((P, P + 2 * T + (1 + len(LEVELS)) * P), np.float32)
    c[:, 0:P] = np.eye(P)
    t = np.arange(T)
    for g, w in enumerate(POOL_WINDOWS):
        at = P + (g // 2) * T
        c[(g % 2) * 64:(g % 2) * 64 + 64, at:at + T] = 1.0 / np.minimum(t + 1, w)
    s, t = np.arange(P)[:, None], np.arange(P)[None, :]
    at = P + 2 * T
    c[:, at:at + P] = (s // BASE == t // BASE) & (s <= t)
    for n, bs in enumerate(LEVELS):
        at += P
        c[:, at:at + P] = (s // bs == t // bs) & (s % bs < bs // 2) & (t % bs >= bs // 2)
    return c


def trunk(nc, x, meta, ffn1_pre, ffn1_post, ffn1_wg, ffn1_wu, ffn1_wd, mix_pre, mix_post, w_in,
          pool_w, pool_scale, conv_w, gla_w2, gla_b2, gla_norm, w_out,
          ffn2_pre, ffn2_post, ffn2_wg, ffn2_wu, ffn2_wd, consts, out):
    SEQ = x.shape[1]
    T = SEQ + NMETA
    DEPTH = w_in.shape[0]
    TAIL = T - 2 * P

    FFN_UNITS = 2 * GROUPS + 4 * len(DOWN_K)
    phases = []
    u0 = 0
    for layer in range(DEPTH):
        for kind in ("ffn1", "mix", "ffn2"):
            last = layer == DEPTH - 1
            phases.append(dict(
                kind=kind, layer=layer, u0=u0, b=len(phases),
                f=2 * layer + (kind == "ffn2"),
                m=layer,
                t_in=NMETA if last and kind == "ffn2" else 0,
                t_out=NMETA if last and kind != "ffn1" else 0))
            u0 += MIX_UNITS if kind == "mix" else FFN_UNITS
    NB = len(phases)

    def weights(ph):
        wg, wu, wd = (ffn1_wg, ffn1_wu, ffn1_wd) if ph["kind"] == "ffn1" else (ffn2_wg, ffn2_wu, ffn2_wd)
        tiled = lambda w: w[ph["layer"]].rearrange("(k p) n -> p k n", p=P)
        return tiled(wg), tiled(wu), tiled(wd)

    ctx = ExitStack()
    with ctx:
        def sb(name, shape, dt=F32):
            return ctx.enter_context(nc.sbuf_tensor(name, shape, dt))

        def sem(name):
            return ctx.enter_context(nc.semaphore(name))

        h = sb("h", [P, KT, T])
        x_hi = sb("x_hi", [P, KT, T], F32R)
        x_lo = sb("x_lo", [P, KT, T], F32R)
        f = sb("f", [P, KT, T])
        raw = sb("raw", [P, RING, UNIT])
        w_hi = sb("w_hi", [P, RING, UNIT], F32R)
        w_lo = sb("w_lo", [P, RING, UNIT], F32R)
        cst = sb("cst", [P, P + 2 * T + (1 + len(LEVELS)) * P])
        ones = sb("ones", [P, T])
        par = sb("par", [P, P])
        r_post = sb("r_post", [P, T])
        r_pre = sb("r_pre", [P, T])
        ms = sb("ms", [P, T])
        nt = sb("nt", [P, T])
        w2 = sb("w2", [NMETA, DEPTH, 256])
        wp = sb("wp", [P, DEPTH, 2, P])
        ident = cst[:, 0:P]
        inv_count = cst[:, P:P + 2 * T].rearrange("p (a t) -> p a t", a=2)
        sq_acc = sb("sq_acc", [P, 2, T])
        sq_new = sb("sq_new", [P, 2, T])
        pre_acc = sb("pre_acc", [P, 2, T])
        small = sb("small", [P, 4, 12])

        def mask(n, rows):
            at = P + 2 * T + n * P
            return cst[0:rows, at:at + rows].bitcast(U32)

        ffn_floats = 2 * FT * T + 8 * T
        PAD = 16
        mix_floats = (5 * 2 + 4 + 3 * 4 + 4 + 4) * T + 1536 + 1024 + 4 * (P + TAIL) + 4 * TAIL \
            + 4 * TAIL + 2 * (2 + T)
        arena_bytes = 4 * max(ffn_floats, mix_floats)
        arena = sb("arena", [P, arena_bytes // 4])
        arena_at = nc.sbuf_base - arena_bytes
        laid = [0]

        def place(name, shape, dt=F32):
            n = 4 * int(np.prod(shape[1:]))
            t = nc.alloc_sbuf_tensor_at(name, shape, dt, offset=arena_at + laid[0])
            laid[0] += n
            assert laid[0] <= arena_bytes, (name, laid[0], arena_bytes)
            return t

        hid_hi = place("hid_hi", [P, FT, T], F32R)
        hid_lo = place("hid_lo", [P, FT, T], F32R)
        gate = place("gate", [P, 2, 2, T])
        up = place("up", [P, 2, 2, T])
        laid[0] = 0
        x_tok = place("x_tok", [P, 2, D])
        meta_tok = place("meta_tok", [NMETA, D])
        par_rows = place("par_rows", [P, P])
        out_tok = place("out_tok", [P, 2, D])
        laid[0] = 0
        q = place("q", [P, 2, T])
        k = place("k", [P, 2, T])
        v = place("v", [P, 4, T])
        b = place("b", [P, 2, T])
        la = place("la", [P, 2, T])
        lt = place("lt", [P, 2, T])
        dec = place("dec", [P, 2, 2, T])
        qd = place("qd", [P, 2, 2, T])
        kd = place("kd", [P, 2, 2, T])
        v_tok = place("v_tok", [P, 3, 512])
        s_diag = place("s_diag", [P, 2, 2, 2, P])
        s_next = place("s_next", [P, 4, P + TAIL])
        s_tail = place("s_tail", [P, 4, TAIL])
        s_last = place("s_last", [TAIL, 2, 2, TAIL])
        g_out = place("g_out", [P, 4, T])
        c_cu = place("c_cu", [P, 4, T])
        z_pad = place("z_pad", [P, 2, 2 + T])
        glow = z_pad[0:NMETA, 0, 2:2 + T]
        y_tmp = la
        inv_dec = lt
        c_b = lt
        y_head = v
        f_flat = f[:, :, :].rearrange("p k t -> p (k t)")
        n_win = 2 * (PAD + T)
        pool_in, win_a, win_b = (f_flat[:, i * n_win:(i + 1) * n_win].rearrange("p (a t) -> p a t", a=2)
                                 for i in range(3))

        ps = ctx.enter_context(nc.psum_tensor("ps", [P, 8, 512], F32))

        raw_in = [sem(f"raw_in{i}") for i in range(RING)]
        unit_hi = sem("unit_hi")
        unit_lo = sem("unit_lo")
        unit_used = sem("unit_used")
        par_in = sem("par_in")
        mix_in = sem("mix_in")
        x_in = sem("x_in")
        zeroed = sem("zeroed")
        ones_set = sem("ones_set")
        ends_tr = sem("ends_tr")
        staged = [sem(f"staged{i}") for i in range(2)]
        par_ready = sem("par_ready")
        h_ready = sem("h_ready")
        xh_ready = sem("xh_ready")
        xl_ready = sem("xl_ready")
        sq_ready = sem("sq_ready")
        pre_sum = sem("pre_sum")
        ss_pre = sem("ss_pre")
        ms_read = sem("ms_read")
        rpre_ready = sem("rpre_ready")
        dve = sem("dve")
        gate_ready = sem("gate_ready")
        silu_done = sem("silu_done")
        up_evac = sem("up_evac")
        hid_mul = sem("hid_mul")
        hid_hi_ready = sem("hid_hi_ready")
        hid_lo_ready = sem("hid_lo_ready")
        pair_out = sem("pair_out")
        sq_pair = sem("sq_pair")
        sq_sum = sem("sq_sum")
        ss_post = sem("ss_post")
        done_out = sem("done_out")
        m_evac = sem("m_evac")
        m_cleared = sem("m_cleared")
        half_done = sem("half_done")
        z_mm = sem("z_mm")
        z_out = sem("z_out")
        lt_step = sem("lt_step")
        dec_arg = sem("dec_arg")
        dec_exp = sem("dec_exp")
        qk_dec = sem("qk_dec")
        job_mm = sem("job_mm")
        vt_mm = sem("vt_mm")
        act_out = sem("act_out")
        act_cp = sem("act_cp")
        cp_out = sem("cp_out")
        g_silu = sem("g_silu")
        pool_win = sem("pool_win")
        pool_own = sem("pool_own")
        pool_mm = sem("pool_mm")
        pool_out = sem("pool_out")
        y_ready = sem("y_ready")
        y_hi = sem("y_hi")
        y_lo = sem("y_lo")
        o_mm = sem("o_mm")
        o_sq = sem("o_sq")
        o_norm = sem("o_norm")
        o_tr = sem("o_tr")

        block = ctx.enter_context(nc.Block())

        C = {}
        rows = [("ffn1_pre", ffn1_pre, KT), ("ffn1_post", ffn1_post, KT), ("mix_pre", mix_pre, KT),
                ("mix_post", mix_post, KT), ("ffn2_pre", ffn2_pre, KT), ("ffn2_post", ffn2_post, KT),
                ("pool_scale", pool_scale, 2), ("conv_w", conv_w, 6), ("gla_b2", gla_b2, 2),
                ("gla_norm", gla_norm, 4)]
        n_rows = 0
        for name, _, per in rows:
            C[name] = (n_rows, per)
            n_rows += DEPTH * per

        def col(name, layer, i):
            base, per = C[name]
            c = base + layer * per + i
            return par[:, c:c + 1]

        def f32(ap):
            return ap.bitcast(F32)

        def last_of(ph, what):
            return ph["u0"] + what + 1 + RING

        UP_UNITS = 2 * GROUPS
        MIX_SIZE = [UNIT] * 4 + [1024] + [UNIT] * 10
        PROJ = ((Q_QK, 0), (Q_V, 2), (C_GLOW, 4), (Q_GOUT, 5), (Q_POOL_CB, 7), (Q_CC_CU, 9))

        @block.sync
        def _(sp):
            def load(slot, value, *copies):
                sp.wait_ge(unit_lo, value)
                for dst, src in copies:
                    sp.dma_start(dst, src).then_inc(raw_in[slot], 16)

            for ph in phases:
                u0, layer = ph["u0"], ph["layer"]
                if ph["kind"] != "mix":
                    wg, wu, wd = weights(ph)

                    def up_unit(j, value, cols):
                        slot = (u0 + j) % RING
                        dst = raw[:, slot].rearrange("p (s k n) -> p s k n", s=2, k=4)
                        ks = slice(4 * (j % 2), 4 * (j % 2) + 4)
                        load(slot, value, (dst[:, 0], wg[:, ks, cols]), (dst[:, 1], wu[:, ks, cols]))

                    for j in range(2):
                        up_unit(j, u0 + j + 1, slice(0, 256))
                    with sp.Fori(0, GROUPS // 2) as i:
                        for j in range(4):
                            up_unit(2 + j, i * 4 + (u0 + 2 + j + 1), bass.ds(i * 512 + 256 + 256 * (j // 2), 256))
                    with sp.Fori(0, KT // 2) as i:
                        k0 = 0
                        for j, nk in enumerate(DOWN_K):
                            slot = (u0 + UP_UNITS + j) % RING
                            dst = raw[:, slot, 0:nk * 256].rearrange("p (k n) -> p k n", k=nk)
                            cols = bass.ds(i * 256, 256)
                            load(slot, i * 4 + (u0 + UP_UNITS + j + 1),
                                 (dst[:, 0:3], wd[:, k0:k0 + 3, cols]), (dst[:, 3:nk], wd[:, k0 + 3:k0 + nk, cols]))
                            k0 += nk
                else:
                    wi = w_in[layer].rearrange("(k p) n -> p k n", p=P)
                    wo = w_out[layer].rearrange("(k p) n -> p k n", p=P)

                    def block_unit(j, w, k0, nk, c0, n):
                        slot = (u0 + j) % RING
                        dst = raw[:, slot, 0:nk * n].rearrange("p (k n) -> p k n", k=nk)
                        half = nk // 2
                        load(slot, u0 + j + 1, (dst[:, 0:half], w[:, k0:k0 + half, c0:c0 + n]),
                             (dst[:, half:nk], w[:, k0 + half:k0 + nk, c0:c0 + n]))
                    for c0, j in PROJ:
                        if c0 == C_GLOW:
                            block_unit(j, wi, 0, 8, c0, P)
                        else:
                            block_unit(j, wi, 0, 4, c0, 512)
                            block_unit(j + 1, wi, 4, 4, c0, 512)
                    for j in range(4):
                        block_unit(11 + j, wo, 4 * (j % 2), 4, 512 * (j // 2), 512)
            for tt in range(2):
                sp.wait_ge(staged[tt], 1)
                sp.dma_start(out[0, tt * P:(tt + 1) * P, :], out_tok[:, tt]).then_inc(done_out, 16)
            sp.wait_ge(done_out, 32)

        @block.scalar
        def _(act):
            for name, src, per in rows:
                r0 = C[name][0]
                if name == "conv_w":
                    by_tile = src.rearrange("l j (a p) -> (l j a) p", p=P)
                else:
                    by_tile = src.rearrange("l (a p) -> (l a) p", p=P)
                act.dma_start(par_rows[r0:r0 + DEPTH * per, :], by_tile).then_inc(par_in, 16)
            act.dma_start(cst[:, :], consts).then_inc(par_in, 16)
            act.dma_start(meta_tok[:, :], meta).then_inc(x_in, 16)
            for tt in range(2):
                act.dma_start(x_tok[:, tt], x[0, tt * P:(tt + 1) * P, :]).then_inc(x_in, 16)
            act.dma_start(w2[:, :, :], gla_w2.rearrange("l r n -> r l n")).then_inc(mix_in, 16)
            act.wait_ge(zeroed, 1)
            for g in range(2):
                act.dma_start(wp[g * 64:g * 64 + 64, :, :, g * 64:g * 64 + 64].rearrange("c l a d -> c (l a) d"),
                              pool_w.rearrange("l (a g) c d -> g c (l a) d", g=2)[g]).then_inc(mix_in, 16)

            def high(slot, n, arrived, free):
                act.wait_ge(raw_in[slot], arrived)
                act.wait_ge(unit_used, free)
                act.activation(w_hi[:, slot, 0:n], raw[:, slot, 0:n], ACT.Copy).then_inc(unit_hi, 1)

            def high_unit(u, n):
                high(u % RING, n, 32 * (u // RING + 1), u + 1)

            def split_h(bnd, gain, layer, t0):
                for kk in range(KT):
                    act.wait_ge(h_ready, 8 * bnd + kk + 1)
                    act.activation(x_hi[:, kk, t0:T], h[:, kk, t0:T], ACT.Copy,
                                   scale=col(gain, layer, kk)).then_inc(xh_ready, 1)
                    act.activation(f[:, kk, t0:T], h[:, kk, t0:T], ACT.Square).then_inc(sq_ready, 1)

            def pair_evac(blk, pair, bank, t0, sem_, used):
                act.wait_ge(sem_, used)
                src = ps[:, bank:bank + 2, 0:T - t0]
                dst = sq_acc if pair == 0 else sq_new
                if pair > 1:
                    act.wait_ge(sq_sum, 3 * blk + pair - 1)
                act.activation(dst[:, :, t0:T], src, ACT.Square).then_inc(sq_pair, 1)
                act.activation(f[:, 2 * pair:2 * pair + 2, t0:T], src, ACT.Copy).then_inc(pair_out, 1)

            for u in range(RING):
                high_unit(u, UNIT)
            act.wait_ge(par_ready, 1)
            for ph in phases:
                u0, layer, bnd, t0 = ph["u0"], ph["layer"], ph["b"], ph["t_in"]
                split_h(bnd, {"ffn1": "ffn1_pre", "mix": "mix_pre", "ffn2": "ffn2_pre"}[ph["kind"]], layer, t0)
                if bnd > 0:
                    high_unit(u0 + 3, UNIT)
                if ph["kind"] != "mix":
                    fi = ph["f"]

                    def group(parity, ua, i4, i32, idx, dst):
                        high(ua % RING, UNIT, i32 + 32 * (ua // RING + 1), i4 + (ua + 1))
                        act.wait_ge(gate_ready, idx)
                        act.activation(gate[:, parity, :, t0:T], gate[:, parity, :, t0:T], ACT.Silu)\
                           .then_inc(silu_done, 1)
                        high((ua + 1) % RING, UNIT, i32 + 32 * ((ua + 1) // RING + 1), i4 + (ua + 2))
                        act.wait_ge(hid_mul, idx)
                        act.activation(dst, up[:, parity, :, t0:T], ACT.Copy).then_inc(hid_hi_ready, 1)

                    group(0, u0 + RING, 0, 0, GROUPS * fi + 1, hid_hi[:, 0:2, t0:T])
                    with act.Fori(0, GROUPS // 2) as i:
                        for g in (1, 2):
                            group(g % 2, u0 + 2 * g + RING, i * 4, i * 32, i * 2 + (GROUPS * fi + g + 1),
                                  hid_hi[:, bass.ds(i * 4 + 2 * g, 2), t0:T])
                    d0 = u0 + UP_UNITS
                    for pair in range(KT // 2):
                        last_pair = pair == KT // 2 - 1
                        for j in range(4):
                            u = d0 + 4 * pair + j + RING
                            if not last_pair:
                                high_unit(u, DOWN_K[j] * 256)
                            elif j < 3 and bnd < NB - 1:
                                high_unit(u, UNIT)
                        pair_evac(bnd, pair, 4 + 2 * (pair % 2), t0, unit_used, last_of(ph, UP_UNITS + 4 * pair + 3))
                else:
                    m, t1 = ph["m"], ph["t_out"]

                    def ahead(j):
                        high_unit(u0 + j + RING, MIX_SIZE[j + RING] if j + RING < MIX_UNITS else UNIT)

                    def decays(j):
                        act.wait_ge(dec_arg, JOBS * m + j + 1)
                        n = T if j < 4 or j == JOBS - 1 else 2 * P
                        if j == 0:
                            act.activation(inv_dec[:, :, :], dec[:, 0], ACT.Exp, scale=-1.0).then_inc(act_cp, 1)
                            act.wait_ge(act_cp, 5 * m + 1)
                        act.activation(dec[:, j % 2, :, 0:n], dec[:, j % 2, :, 0:n], ACT.Exp).then_inc(dec_exp, 1)

                    for j in range(6):
                        ahead(j)
                    act.wait_ge(z_out, m + 1)
                    act.activation(lt[:, :, :], la[:, :, :], ACT.Abs).then_inc(lt_step, 1)
                    act.wait_ge(lt_step, 3 * m + 1)
                    act.activation(lt[:, :, :], lt[:, :, :], ACT.Exp, scale=-1.0).then_inc(lt_step, 1)
                    act.wait_ge(lt_step, 3 * m + 2)
                    act.activation(lt[:, :, :], lt[:, :, :], ACT.Ln, bias=1.0).then_inc(lt_step, 1)
                    ahead(6)
                    decays(0)
                    decays(1)
                    ahead(7)
                    decays(2)
                    ahead(8)
                    decays(3)
                    ahead(9)
                    ahead(10)
                    act.wait_ge(vt_mm, m + 1)
                    act.activation(v_tok[:, 0:2, :], ps[:, 0:2, :], ACT.Copy).then_inc(act_cp, 1)
                    act.activation(v_tok[0:TAIL, 2, :], ps[0:TAIL, 2, :], ACT.Copy).then_inc(act_out, 1)
                    act.wait_ge(unit_used, last_of(ph, 10))

                    def high_y(n, kk, src):
                        act.wait_ge(y_ready, 8 * m + n)
                        act.activation(x_hi[:, kk, :], src, ACT.Copy).then_inc(y_hi, 1)
                    for a in range(2):
                        high_y(a + 1, 2 + a, c_cu[:, a, :])
                    decays(4)
                    for a in range(2):
                        high_y(a + 3, a, y_tmp[:, a, :])
                    for j in range(5, JOBS):
                        decays(j)
                    act.activation(g_out[:, :, :], g_out[:, :, :], ACT.Silu).then_inc(g_silu, 1)
                    act.wait_ge(cp_out, 6 * m + 6)
                    act.wait_ge(job_mm, JOBS * m + 7)
                    for c in range(2):
                        src = ps[0:64, 2 * c:2 * c + 2, 0:P].rearrange("p b (a t) -> p b a t", a=2)
                        act.activation(s_diag[0:64, c, :, :, 64:P], src, ACT.Copy)\
                           .then_inc((act_cp, act_out)[c], 1)
                    act.wait_ge(job_mm, JOBS * m + 8)
                    for pr in range(2):
                        act.activation(s_next[:, pr:4:2, 0:P],
                                       ps[:, 4 + pr, 0:2 * P].rearrange("p (a t) -> p a t", a=2), ACT.Copy)\
                           .then_inc((act_cp, act_out)[pr], 1)
                    act.wait_ge(job_mm, JOBS * m + 9)
                    for pr in range(2):
                        both = ps[:, pr, 0:4 * TAIL].rearrange("p (c a t) -> p c a t", c=2, a=2)
                        act.activation(s_next[:, pr:4:2, P:P + TAIL], both[:, 0], ACT.Copy).then_inc(act_cp, 1) \
                            if pr == 0 else act.activation(s_next[:, pr:4:2, P:P + TAIL], both[:, 0], ACT.Copy)
                        last = act.activation(s_tail[:, pr:4:2, :], both[:, 1], ACT.Copy)
                    last.then_inc(act_out, 1)
                    act.wait_ge(o_mm, m + 1)
                    sq_o = qd[:, :, :, :].rearrange("p a b t -> p (a b t)")
                    act.activation(sq_o[:, 0:1024].rearrange("p (c n) -> p c n", c=2), ps[:, 4:6, :], ACT.Square)
                    act.activation(kd[:, :, :, :].rearrange("p a b t -> p (a b t)")[0:TAIL, 0:512], ps[0:TAIL, 6, :],
                                   ACT.Square).then_inc(o_sq, 1)
                    for a in range(4):
                        high_y(a + 5, 4 + a, y_head[:, a, :])
                    ahead(11)
                    ahead(12)
                    for pair in range(2):
                        pair_evac(bnd, pair, 2 * pair, t1, unit_used, last_of(ph, 12))
                    ahead(13)
                    pair_evac(bnd, 2, 4, t1, half_done, m + 1)
                    pair_evac(bnd, 3, 6, t1, unit_used, last_of(ph, 14))
            act.wait_ge(ends_tr, 3)
            act.activation(out_tok[:, 0, :].rearrange("p (a n) -> p a n", a=2), ps[:, 0:2, :], ACT.Copy)\
               .then_inc(staged[0], 1)

        @block.vector
        def _(v_):
            own = [0]

            def mark(ins):
                ins.then_inc(dve, 1)
                own[0] += 1
                return own[0]

            def low(slot, n, count):
                v_.wait_ge(unit_hi, count)
                v_.tensor_tensor(w_lo[:, slot, 0:n], raw[:, slot, 0:n], f32(w_hi[:, slot, 0:n]), ALU.subtract)\
                  .then_inc(unit_lo, 1)

            def low_unit(u, n):
                low(u % RING, n, u + 1)

            def rsqrt(src, n, mean, tmp, dst, read=None):
                ins = v_.tensor_scalar(mean, src, 1.0 / n, EPS, ALU.mult, ALU.add)
                c = mark(ins)
                v_.wait_ge(dve, c)
                if read is not None:
                    v_.sem_inc(read, 1)
                c = mark(v_.tensor_scalar(dst.bitcast(I32), mean.bitcast(I32), -0.5, MAGIC, ALU.mult, ALU.add))
                for _ in range(3):
                    v_.wait_ge(dve, c)
                    c = mark(v_.tensor_tensor(tmp, dst, dst, ALU.mult))
                    v_.wait_ge(dve, c)
                    c = mark(v_.scalar_tensor_tensor(tmp, tmp, -0.5, mean, ALU.mult, ALU.mult))
                    v_.wait_ge(dve, c)
                    c = mark(v_.scalar_tensor_tensor(dst, tmp, 1.5, dst, ALU.add, ALU.mult))
                v_.wait_ge(dve, c)

            def tok(r, a, t0):
                return r[:, t0:T].unsqueeze(1).to_broadcast([P, a, T - t0])

            def new_h(bnd, post, pre, layer, layer_pre, t0, final):
                def low_x(kk):
                    v_.wait_ge(xh_ready, 8 * bnd + kk + 1)
                    v_.scalar_tensor_tensor(x_lo[:, kk, t0:T], h[:, kk, t0:T], col(pre, layer_pre, kk),
                                            f32(x_hi[:, kk, t0:T]), ALU.mult, ALU.subtract).then_inc(xl_ready, 1)
                c = {}

                def scale(kk, n):
                    v_.wait_ge(pair_out, 4 * (bnd - 1) + kk // 2 + 1)
                    c[kk] = c[kk + n - 1] = mark(v_.tensor_tensor(
                        f[:, kk:kk + n, t0:T], f[:, kk:kk + n, t0:T], tok(r_post, n, t0), ALU.mult))

                def add(kk):
                    v_.wait_ge(dve, c[kk])
                    v_.scalar_tensor_tensor(h[:, kk, t0:T], f[:, kk, t0:T], col(post, layer, kk),
                                            h[:, kk, t0:T], ALU.mult, ALU.add).then_inc(h_ready, 1)
                scale(0, 1)
                scale(1, 1)
                add(0)
                for kk in range(1, KT):
                    if kk % 2 and kk + 1 < KT:
                        scale(kk + 1, 2)
                    add(kk)
                    if kk > 1 and not final:
                        low_x(kk - 2)
                if not final:
                    low_x(KT - 2)
                    low_x(KT - 1)

            v_.memset(ones[:, :], 1.0).then_inc(ones_set, 1)
            for _ in range(RING):
                v_.sem_inc(unit_lo, 1)
            v_.sem_inc(up_evac, 1)
            v_.sem_inc(up_evac, 1)
            v_.wait_ge(ends_tr, 1)
            c = mark(v_.tensor_copy(par[:, 0:n_rows], ps[:, 7, T:T + n_rows]))
            v_.wait_ge(dve, c)
            for name in ("ffn1_post", "ffn2_post"):
                cs = slice(C[name][0], C[name][0] + DEPTH * KT)
                c = mark(v_.tensor_scalar(par[:, cs], par[:, cs], 0.5, None, ALU.mult))
            v_.wait_ge(dve, c)
            v_.sem_inc(par_ready, 1)
            v_.wait_ge(ends_tr, 2)
            for kk in range(KT):
                v_.tensor_copy(h[:, kk, :], ps[:, kk, 0:T]).then_inc(h_ready, 1)
            for kk in range(KT):
                v_.wait_ge(xh_ready, kk + 1)
                v_.scalar_tensor_tensor(x_lo[:, kk, :], h[:, kk, :], col("ffn1_pre", 0, kk),
                                        f32(x_hi[:, kk, :]), ALU.mult, ALU.subtract).then_inc(xl_ready, 1)
            for u in range(RING):
                low_unit(u, UNIT)

            POST = {"ffn1": "ffn1_post", "mix": "mix_post", "ffn2": "ffn2_post"}
            PRE = {"ffn1": "ffn1_pre", "mix": "mix_pre", "ffn2": "ffn2_pre"}
            for ph in phases:
                u0, layer, bnd, t0 = ph["u0"], ph["layer"], ph["b"], ph["t_in"]
                if bnd > 0:
                    low_unit(u0 + 3, UNIT)

                def pre_rms():
                    v_.wait_ge(ss_pre, bnd + 1)
                    rsqrt(ps[:, 4, 0:T - t0], D, ms[:, t0:T], nt[:, t0:T], r_pre[:, t0:T], read=ms_read)

                def sum_squares(pair, ts):
                    v_.wait_ge(sq_pair, 4 * bnd + pair + 1)
                    v_.tensor_tensor(sq_acc[:, :, ts:T], sq_acc[:, :, ts:T], sq_new[:, :, ts:T], ALU.add)\
                      .then_inc(sq_sum, 1)
                    if pair == 2:
                        v_.wait_ge(sq_sum, 3 * bnd + 2)
                        v_.tensor_tensor(sq_acc[:, 0, ts:T], sq_acc[:, 0, ts:T], sq_acc[:, 1, ts:T], ALU.add)\
                          .then_inc(sq_sum, 1)

                if ph["kind"] != "mix":
                    fi = ph["f"]

                    def group(parity, ua, i4, idx):
                        low(ua % RING, UNIT, i4 + (ua + 1))
                        v_.wait_ge(unit_used, i4 + (ua + 2))
                        v_.wait_ge(hid_lo_ready, idx)
                        bank = 4 * parity
                        v_.tensor_tensor(gate[:, parity, :, t0:T], ps[:, bank:bank + 2, 0:T - t0],
                                         tok(r_pre, 2, t0), ALU.mult).then_inc(gate_ready, 1)
                        v_.tensor_tensor(up[:, parity, :, t0:T], ps[:, bank + 2:bank + 4, 0:T - t0],
                                         tok(r_pre, 2, t0), ALU.mult).then_inc(up_evac, 1)
                        low((ua + 1) % RING, UNIT, i4 + (ua + 2))

                    pre_rms()
                    group(0, u0 + RING, 0, GROUPS * fi + 1)
                    with v_.Fori(0, GROUPS // 2) as i:
                        for g in (1, 2):
                            group(g % 2, u0 + 2 * g + RING, i * 4, i * 2 + (GROUPS * fi + g + 1))
                    d0 = u0 + UP_UNITS
                    for pair in range(KT // 2):
                        last_pair = pair == KT // 2 - 1
                        for j in range(4):
                            u = d0 + 4 * pair + j + RING
                            if not last_pair:
                                low_unit(u, DOWN_K[j] * 256)
                            elif j < 3 and bnd < NB - 1:
                                low_unit(u, UNIT)
                        if pair in (1, 2):
                            sum_squares(pair, t0)
                    t_end = t0
                else:
                    m, t_end = ph["m"], ph["t_out"]

                    def ahead(j):
                        low_unit(u0 + j + RING, MIX_SIZE[j + RING] if j + RING < MIX_UNITS else UNIT)

                    def by_block(x_, bs, n):
                        return x_[:, :, 0:n].rearrange("p a (n s) -> p a n s", s=bs)

                    def exponents(j):
                        if j >= 2:
                            v_.wait_ge(qk_dec, JOBS * m + j - 1)
                        d = dec[:, j % 2]
                        if j == 0:
                            bb = by_block(b, BASE, T)
                            ref = bb[:, :, :, 0:1].to_broadcast([P, 2, T // BASE, BASE])
                            v_.tensor_tensor(by_block(d, BASE, T), bb, ref, ALU.subtract).then_inc(dec_arg, 1)
                        elif j < JOBS - 1:
                            bs = 2 * BASE << (j - 1)
                            n = T if T % bs == 0 else 2 * P
                            bb, dd, hf = by_block(b, bs, n), by_block(d, bs, n), bs // 2
                            ref = bb[:, :, :, hf - 1:hf].to_broadcast([P, 2, n // bs, hf])
                            v_.tensor_tensor(dd[:, :, :, 0:hf], ref, bb[:, :, :, 0:hf], ALU.subtract)
                            v_.tensor_tensor(dd[:, :, :, hf:bs], bb[:, :, :, hf:bs], ref, ALU.subtract)\
                              .then_inc(dec_arg, 1)
                        else:
                            ref = b[:, :, 2 * P - 1:2 * P]
                            v_.tensor_tensor(d[:, :, 0:2 * P], ref.to_broadcast([P, 2, 2 * P]), b[:, :, 0:2 * P],
                                             ALU.subtract)
                            v_.tensor_tensor(d[:, :, 2 * P:T], b[:, :, 2 * P:T], ref.to_broadcast([P, 2, TAIL]),
                                             ALU.subtract).then_inc(dec_arg, 1)

                    def take_scores(j):
                        v_.wait_ge(job_mm, JOBS * m + j + 1)
                        v_.wait_ge(m_cleared, m + 1)
                        bank = 0 if j in (2, 4) else 4
                        src = ps[:, bank:bank + 4, 0:2 * P].rearrange("p b (a t) -> p b a t", a=2)
                        dst = s_diag[:, :, :, :, :].rearrange("p c b a t -> p (c b) a t")
                        if j:
                            v_.wait_ge(cp_out, 6 * m + j)
                        last = v_.copy_predicated(dst, mask(j, P).unsqueeze(1).unsqueeze(1).to_broadcast([P, 4, 2, P]), src)
                        if j < 4:
                            last = v_.copy_predicated(
                                s_last[:, :, :, :],
                                mask(j, TAIL).unsqueeze(1).unsqueeze(1).to_broadcast([TAIL, 2, 2, TAIL]),
                                ps[0:TAIL, bank:bank + 2, 2 * P:2 * P + 2 * TAIL].rearrange("p b (a t) -> p b a t", a=2))
                        last.then_inc(cp_out, 1)

                    def low_y(n, kk, src):
                        v_.wait_ge(y_hi, 8 * m + n)
                        v_.tensor_tensor(x_lo[:, kk, :], src, f32(x_hi[:, kk, :]), ALU.subtract).then_inc(y_lo, 1)

                    ahead(0)
                    pre_rms()
                    ahead(1)
                    v_.wait_ge(unit_used, last_of(ph, 1))
                    v_.scalar_tensor_tensor(q[:, :, :], ps[:, 0:2, 0:T], 0.125, tok(r_pre, 2, 0), ALU.mult, ALU.mult)
                    v_.tensor_tensor(k[:, :, :], ps[:, 2:4, 0:T], tok(r_pre, 2, 0), ALU.mult).then_inc(m_evac, 1)
                    ahead(2)
                    ahead(3)
                    v_.wait_ge(unit_used, last_of(ph, 3))
                    v_.tensor_tensor(v[:, :, :], ps[:, 4:8, 0:T], tok(r_pre, 4, 0), ALU.mult).then_inc(m_evac, 1)
                    ahead(4)
                    v_.wait_ge(unit_used, last_of(ph, 4))
                    v_.tensor_tensor(glow, ps[0:NMETA, 0, 0:T], r_pre[0:NMETA, :], ALU.mult).then_inc(m_evac, 1)
                    ahead(5)
                    v_.wait_ge(z_mm, m + 1)
                    for a in range(2):
                        last = v_.tensor_scalar(la[:, a, :], ps[:, 1 + a, 0:T], col("gla_b2", layer, a), None, ALU.add)
                    last.then_inc(z_out, 1)
                    v_.wait_ge(lt_step, 3 * m + 3)
                    flat = lambda x_: x_[:, :, :].rearrange("p a t -> p (a t)")
                    c = mark(v_.scalar_tensor_tensor(flat(la), flat(la), 0.0, flat(lt), ALU.min, ALU.subtract))
                    v_.wait_ge(dve, c)
                    c = mark(v_.tensor_scalar(flat(la), flat(la), 1.0 / 16, LOG_DECAY_MIN, ALU.mult, ALU.max))
                    v_.wait_ge(dve, c)
                    for a in range(2):
                        c = mark(v_.tensor_tensor_scan(b[:, a, :], ones[:, 0:T], la[:, a, :], 0.0, ALU.mult, ALU.add))
                    ahead(6)
                    v_.wait_ge(unit_used, last_of(ph, 6))
                    v_.tensor_tensor(g_out[:, :, :], ps[:, 4:8, 0:T], tok(r_pre, 4, 0), ALU.mult).then_inc(m_evac, 1)
                    v_.wait_ge(dve, c)
                    exponents(0)
                    exponents(1)
                    ahead(7)
                    exponents(2)
                    v_.wait_ge(unit_used, last_of(ph, 8))
                    v_.wait_ge(m_cleared, m + 1)
                    v_.tensor_tensor(pool_in[:, :, PAD:PAD + T], ps[:, 0:2, 0:T], tok(r_pre, 2, 0), ALU.mult)
                    v_.tensor_tensor(c_b[:, :, :], ps[:, 2:4, 0:T], tok(r_pre, 2, 0), ALU.mult).then_inc(m_evac, 1)
                    ahead(8)
                    exponents(3)
                    ahead(9)
                    v_.wait_ge(unit_used, last_of(ph, 10))
                    c = mark(v_.tensor_tensor(c_cu[:, :, :], ps[:, 4:8, 0:T], tok(r_pre, 4, 0), ALU.mult))
                    v_.wait_ge(dve, c)
                    v_.sem_inc(m_evac, 1)
                    ahead(10)
                    c = mark(v_.tensor_tensor(z_pad[:, :, 2:2 + T], c_cu[:, 0:2, :], c_cu[:, 2:4, :], ALU.mult))
                    v_.wait_ge(dve, c)
                    for a in range(2):
                        c = mark(v_.tensor_scalar(c_cu[:, a, :], z_pad[:, a, 2:2 + T], col("conv_w", layer, 4 + a),
                                                  None, ALU.mult))
                    for j in (1, 0):
                        for a in range(2):
                            v_.wait_ge(dve, c - 1)
                            c = mark(v_.scalar_tensor_tensor(c_cu[:, a, :], z_pad[:, a, j:j + T],
                                                             col("conv_w", layer, 2 * j + a), c_cu[:, a, :],
                                                             ALU.mult, ALU.add))
                    for a in range(2):
                        v_.wait_ge(dve, c - 1 + a)
                        v_.tensor_tensor(c_cu[:, a, :], c_cu[:, a, :], c_b[:, a, :], ALU.mult).then_inc(y_ready, 1)
                    for a in range(2):
                        low_y(a + 1, 2 + a, c_cu[:, a, :])
                    exponents(4)
                    take_scores(0)
                    v_.wait_ge(pool_mm, m + 1)
                    for a in range(2):
                        v_.tensor_scalar(y_tmp[:, a, :], ps[:, a, 0:T], col("pool_scale", layer, a), None, ALU.mult)\
                          .then_inc(y_ready, 1)
                    for a in range(2):
                        low_y(a + 3, a, y_tmp[:, a, :])
                    exponents(5)
                    take_scores(1)
                    exponents(6)
                    take_scores(2)
                    exponents(7)
                    take_scores(3)
                    exponents(8)
                    take_scores(4)
                    take_scores(5)
                    v_.wait_ge(o_sq, m + 1)
                    sq_o = qd[:, :, :, :].rearrange("p a b t -> p (a b t)")
                    v_.tensor_reduce(small[:, 0, 0:8], sq_o[:, 0:1024].rearrange("p (a n) -> p a n", a=8),
                                     mybir.AxisListType.X, ALU.add)
                    c = mark(v_.tensor_reduce(
                        small[0:TAIL, 0, 8:12],
                        kd[:, :, :, :].rearrange("p a b t -> p (a b t)")[0:TAIL, 0:512].rearrange("p (a n) -> p a n", a=4),
                        mybir.AxisListType.X, ALU.add))
                    v_.wait_ge(dve, c)
                    rsqrt(small[:, 0], P, small[:, 1], small[:, 2], small[:, 3])
                    for ch in range(3):
                        n = P if ch < 2 else TAIL
                        last = v_.tensor_tensor(
                            v_tok[0:n, ch, :].rearrange("p (a e) -> p a e", a=4),
                            ps[0:n, 4 + ch, :].rearrange("p (a e) -> p a e", a=4),
                            small[0:n, 3, 4 * ch:4 * ch + 4].unsqueeze(2).to_broadcast([n, 4, P]), ALU.mult)
                    last.then_inc(o_norm, 1)
                    v_.wait_ge(o_tr, m + 1)
                    v_.wait_ge(g_silu, m + 1)
                    for a in range(4):
                        v_.scalar_tensor_tensor(y_head[:, a, :], ps[:, 4 + a, 0:T], col("gla_norm", layer, a),
                                                g_out[:, a, :], ALU.mult, ALU.mult).then_inc(y_ready, 1)
                        if a > 0:
                            low_y(a + 4, 3 + a, y_head[:, a - 1, :])
                    low_y(8, 7, y_head[:, 3, :])
                    ahead(11)
                    ahead(12)
                    sum_squares(1, t_end)
                    ahead(13)
                    sum_squares(2, t_end)
                v_.wait_ge(ss_post, bnd + 1)
                rsqrt(ps[:, 3, 0:T - t_end], D, ms[:, t_end:T], nt[:, t_end:T], r_post[:, t_end:T])
                final = bnd == NB - 1
                nx = phases[min(bnd + 1, NB - 1)]
                new_h(bnd + 1, POST[ph["kind"]], PRE[nx["kind"]], layer, nx["layer"], t_end, final)
            v_.wait_ge(ends_tr, 4)
            v_.tensor_copy(out_tok[:, 1, :].rearrange("p (a n) -> p a n", a=2), ps[:, 2:4, :]).then_inc(staged[1], 1)

        @block.gpsimd
        def _(pool):
            pool.memset(wp[:, :, :, :], 0.0).then_inc(zeroed, 1)
            pool.memset(small[:, :, :], 1.0)
            pool.sem_inc(hid_lo_ready, 1)
            pool.sem_inc(hid_lo_ready, 1)
            for ph in phases:
                bnd, t0 = ph["b"], ph["t_in"]
                for n, (a0, a1) in enumerate(((f[:, 0:2], f[:, 2:4]), (pre_acc, f[:, 4:6]), (pre_acc, f[:, 6:8]))):
                    pool.wait_ge(sq_ready, 8 * bnd + 2 * n + 4)
                    if n:
                        pool.wait_ge(pre_sum, 4 * bnd + n)
                    pool.tensor_tensor(pre_acc[:, :, t0:T], a0[:, :, t0:T], a1[:, :, t0:T], ALU.add).then_inc(pre_sum, 1)
                pool.wait_ge(pre_sum, 4 * bnd + 3)
                pool.tensor_tensor(pre_acc[:, 0, t0:T], pre_acc[:, 0, t0:T], pre_acc[:, 1, t0:T], ALU.add)\
                    .then_inc(pre_sum, 1)
                if ph["kind"] != "mix":
                    fi = ph["f"]

                    def group(parity, idx, dst_hi, dst_lo):
                        pool.wait_ge(silu_done, idx)
                        pool.wait_ge(up_evac, idx + 2)
                        pool.tensor_tensor(up[:, parity, :, t0:T], gate[:, parity, :, t0:T],
                                           up[:, parity, :, t0:T], ALU.mult).then_inc(hid_mul, 1)
                        pool.wait_ge(hid_hi_ready, idx)
                        pool.tensor_tensor(dst_lo, up[:, parity, :, t0:T], f32(dst_hi), ALU.subtract)\
                            .then_inc(hid_lo_ready, 1)

                    group(0, GROUPS * fi + 1, hid_hi[:, 0:2, t0:T], hid_lo[:, 0:2, t0:T])
                    with pool.Fori(0, GROUPS // 2) as i:
                        for g in (1, 2):
                            tiles = bass.ds(i * 4 + 2 * g, 2)
                            group(g % 2, i * 2 + (GROUPS * fi + g + 1), hid_hi[:, tiles, t0:T], hid_lo[:, tiles, t0:T])
                else:
                    m = ph["m"]
                    pool.wait_ge(pre_sum, 4 * bnd + 4)
                    pool.memset(s_diag[:, :, :, :, :], 0.0)
                    pool.memset(s_last[:, :, :, :], 0.0)
                    pool.memset(z_pad[:, :, 0:2], 0.0)
                    pool.memset(qd[:, 1], 0.0)
                    pool.memset(kd[:, 1], 0.0)
                    for w in (pool_in, win_a, win_b):
                        last = pool.memset(w[:, :, 0:PAD], 0.0)
                    last.then_inc(m_cleared, 1)
                    pool.wait_ge(m_cleared, m + 1)

                    def with_decays(j):
                        pool.wait_ge(dec_exp, JOBS * m + j + 1)
                        if j >= 2:
                            pool.wait_ge(job_mm, JOBS * m + j - 1)
                        d, qj, kj = dec[:, j % 2], qd[:, j % 2], kd[:, j % 2]
                        if j == 0:
                            pool.tensor_tensor(qj, q[:, :, :], d, ALU.mult)
                            pool.tensor_tensor(kj, k[:, :, :], inv_dec[:, :, :], ALU.mult).then_inc(qk_dec, 1)
                            return
                        if j < JOBS - 1:
                            bs = 2 * BASE << (j - 1)
                            n, hf = (T if T % bs == 0 else 2 * P), bs // 2
                            by = lambda x_: x_[:, :, 0:n].rearrange("p a (n s) -> p a n s", s=bs)
                            lt_, rt = (lambda x_: by(x_)[:, :, :, 0:hf]), (lambda x_: by(x_)[:, :, :, hf:bs])
                        else:
                            lt_, rt = (lambda x_: x_[:, :, 0:2 * P]), (lambda x_: x_[:, :, 2 * P:T])
                        pool.tensor_tensor(rt(qj), rt(q), rt(d), ALU.mult)
                        pool.tensor_tensor(lt_(kj), lt_(k), lt_(d), ALU.mult).then_inc(qk_dec, 1)

                    with_decays(0)
                    with_decays(1)
                    with_decays(2)
                    pool.wait_ge(m_evac, 6 * m + 5)
                    step = [8 * m]

                    def own(ins):
                        ins.then_inc(pool_own, 1)
                        step[0] += 1
                        pool.wait_ge(pool_own, step[0])
                    now = slice(PAD, PAD + T)
                    back = lambda n: slice(PAD - n, PAD - n + T)
                    lo_, hi_ = slice(0, 64), slice(64, P)
                    own(pool.tensor_tensor(win_a[:, :, now], pool_in[:, :, now], pool_in[:, :, back(1)], ALU.add))
                    own(pool.tensor_tensor(win_b[:, :, now], win_a[:, :, now], win_a[:, :, back(2)], ALU.add))
                    own(pool.tensor_tensor(y_tmp[lo_, 0, :], win_a[lo_, 0, now], inv_count[lo_, 0], ALU.mult))
                    own(pool.tensor_tensor(y_tmp[hi_, 0, :], win_b[hi_, 0, now], inv_count[hi_, 0], ALU.mult))
                    own(pool.tensor_tensor(win_a[:, 1, now], win_b[:, 1, now], win_b[:, 1, back(4)], ALU.add))
                    own(pool.tensor_tensor(y_tmp[lo_, 1, :], win_a[lo_, 1, now], inv_count[lo_, 1], ALU.mult))
                    own(pool.tensor_tensor(win_b[hi_, 1, now], win_a[hi_, 1, now], win_a[hi_, 1, back(8)], ALU.add))
                    own(pool.tensor_tensor(y_tmp[hi_, 1, :], win_b[hi_, 1, now], inv_count[hi_, 1], ALU.mult))
                    pool.tensor_tensor(y_tmp[:, :, :], y_tmp[:, :, :], pool_in[:, :, now], ALU.subtract)\
                        .then_inc(pool_win, 1)
                    assert step[0] == 8 * (m + 1)
                    for j in range(3, JOBS):
                        with_decays(j)

        @block.tensor
        def _(pe):
            def mm3(out_, wh, wl, xh, xl, first, last):
                pe.matmul(out_, wh, xh, start=first, stop=False)
                pe.matmul(out_, wh, xl, start=False, stop=False)
                return pe.matmul(out_, wl, xh, start=False, stop=last)

            def unit(slot, count, view, k_list, m_list, bank, xs, t0, k_first, k_last, per_k=None, m_outer=False,
                     half=None):
                pe.wait_ge(unit_lo, count)
                xh, xl = xs
                order = [(kk, mm) for kk in range(len(k_list)) for mm in m_list]
                if m_outer:
                    h_ = len(m_list) // 2
                    order = [(kk, mm) for ms_ in (m_list[:h_], m_list[h_:]) for kk in range(len(k_list)) for mm in ms_]
                waited = -1
                for n, (kk, mm) in enumerate(order):
                    kg = k_list[kk]
                    if per_k is not None and kk > waited:
                        pe.wait_ge(*per_k(kg))
                        waited = kk
                    ins = mm3(ps[:, bank + mm, 0:T - t0], view(w_hi, kk, mm), view(w_lo, kk, mm),
                              xh[:, kg, t0:T], xl[:, kg, t0:T], kg == k_first, kg == k_last)
                    if half is not None and n == len(order) // 2 - 1:
                        ins.then_inc(half, 1)
                ins.then_inc(unit_used, 1)

            def up_view(slot):
                def view(w, kk, mm):
                    return w[:, slot].rearrange("p (s k n) -> p s k n", s=2, k=4)[:, mm // 2, kk, (mm % 2) * P:(mm % 2 + 1) * P]
                return view

            def k_view(slot, nk, n):
                def view(w, kk, mm):
                    return w[:, slot, 0:nk * n].rearrange("p (k n) -> p k n", k=nk)[:, kk, mm * P:(mm + 1) * P]
                return view

            def sum_h(bnd, t0):
                pe.wait_ge(pre_sum, 4 * bnd + 4)
                pe.matmul(ps[:, 4, 0:T - t0], ones[:, 0:P], pre_acc[:, 0, t0:T], start=True, stop=True)\
                  .then_inc(ss_pre, 1)

            def sum_f_most(blk, t0):
                pe.wait_ge(sq_sum, 3 * blk + 3)
                pe.matmul(ps[:, 3, 0:T - t0], ones[:, 0:P], sq_acc[:, 0, t0:T], start=True, stop=False)

            def sum_f_rest(blk, t0):
                pe.wait_ge(sq_pair, 4 * blk + 4)
                pe.matmul(ps[:, 3, 0:T - t0], ones[:, 0:P], sq_new[:, 0, t0:T], start=False, stop=False)
                pe.matmul(ps[:, 3, 0:T - t0], ones[:, 0:P], sq_new[:, 1, t0:T], start=False, stop=True)\
                  .then_inc(ss_post, 1)

            for _ in range(RING):
                pe.sem_inc(unit_used, 1)
            pe.wait_ge(par_in, 16 * (len(rows) + 1))
            pe.transpose(ps[:, 7, T:T + n_rows], par_rows[0:n_rows, :], ident[0:n_rows, 0:n_rows]).then_inc(ends_tr, 1)
            pe.wait_ge(x_in, 48)
            for kk in range(KT):
                if kk == KT - 1:
                    pe.wait_ge(par_ready, 1)
                pe.transpose(ps[:, kk, 0:NMETA], meta_tok[:, kk * P:(kk + 1) * P], ident[0:NMETA, 0:NMETA])
                for tt in range(2):
                    last = pe.transpose(ps[:, kk, NMETA + tt * P:NMETA + (tt + 1) * P],
                                        x_tok[:, tt, kk * P:(kk + 1) * P], ident)
            last.then_inc(ends_tr, 1)

            pe.wait_ge(ones_set, 1)
            for ph in phases:
                u0, layer, bnd, t0 = ph["u0"], ph["layer"], ph["b"], ph["t_in"]
                xs = (x_hi, x_lo)
                x_tile = lambda kg: (xl_ready, 8 * bnd + kg + 1)
                if ph["kind"] != "mix":
                    fi = ph["f"]

                    def group(parity, ja, i4, idx, per_k=None):
                        pe.wait_ge(up_evac, idx)
                        for j in range(2):
                            u = u0 + ja + j
                            unit(u % RING, i4 + (u + 1 + RING), up_view(u % RING), range(4 * j, 4 * j + 4), range(4),
                                 4 * parity, xs, t0, 0, KT - 1, per_k)

                    group(0, 0, 0, GROUPS * fi + 1, x_tile)
                    sum_h(bnd, t0)
                    pe.wait_ge(ms_read, bnd + 1)
                    with pe.Fori(0, GROUPS // 2) as i:
                        for g in (1, 2):
                            group(g % 2, 2 * g, i * 4, i * 2 + (GROUPS * fi + g + 1))
                    d0 = u0 + UP_UNITS
                    hid = (hid_hi, hid_lo)
                    pe.wait_ge(up_evac, GROUPS * fi + GROUPS + 1)

                    def hid_tile(kg):
                        return (hid_lo_ready, GROUPS * fi + kg // 2 + 1 + 2)
                    for pair in range(KT // 2):
                        if pair >= 2:
                            pe.wait_ge(pair_out, 4 * bnd + pair - 1)
                        k0 = 0
                        for j, nk in enumerate(DOWN_K):
                            u = d0 + 4 * pair + j
                            unit(u % RING, u + 1 + RING, k_view(u % RING, nk, 256), range(k0, k0 + nk), range(2),
                                 4 + 2 * (pair % 2), hid, t0, 0, FT - 1, hid_tile if pair == 0 else None)
                            k0 += nk
                            if pair == 3 and j == 2:
                                sum_f_most(bnd, t0)
                    sum_f_rest(bnd, t0)
                else:
                    m, t1 = ph["m"], ph["t_out"]

                    def proj(j, bank, per_k=None):
                        for jj in range(2):
                            proj_unit(j + jj, jj, bank, per_k)

                    def proj_unit(j, half_, bank, per_k=None):
                        u = u0 + j
                        unit(u % RING, u + 1 + RING, k_view(u % RING, 4, 512), range(4 * half_, 4 * half_ + 4), range(4),
                             bank, xs, 0, 0, KT - 1, per_k)

                    proj(0, 0, x_tile)
                    sum_h(bnd, 0)
                    pe.wait_ge(ms_read, bnd + 1)
                    proj(2, 4)
                    pe.wait_ge(m_evac, 6 * m + 1)
                    u = u0 + 4
                    unit(u % RING, u + 1 + RING, k_view(u % RING, 8, P), range(8), range(1), 0, xs, 0, 0, KT - 1)
                    pe.wait_ge(m_evac, 6 * m + 2)
                    proj_unit(5, 0, 4)
                    pe.wait_ge(m_evac, 6 * m + 3)
                    pe.wait_ge(mix_in, 48)
                    for a in range(2):
                        last = pe.matmul(ps[:, 1 + a, 0:T], w2[:, layer, a * P:(a + 1) * P], glow,
                                         start=True, stop=True)
                    last.then_inc(z_mm, 1)
                    proj_unit(6, 1, 4)
                    pe.wait_ge(z_out, m + 1)
                    proj(7, 0)
                    pe.wait_ge(m_evac, 6 * m + 4)
                    proj(9, 4)
                    pe.wait_ge(m_evac, 6 * m + 5)
                    for hh in range(HEADS):
                        for ch in range(2):
                            pe.transpose(ps[:, ch, hh * P:(hh + 1) * P], v[:, hh, ch * P:(ch + 1) * P], ident)
                        last = pe.matmul(ps[0:TAIL, 2, hh * P:(hh + 1) * P], v[:, hh, 2 * P:T], ident,
                                         start=True, stop=True)
                    last.then_inc(vt_mm, 1)

                    def job(j, bank):
                        pe.wait_ge(qk_dec, JOBS * m + j + 1)
                        for a in range(2):
                            for pr in range(2):
                                rows_ = slice(pr * 64, pr * 64 + 64)
                                kk, qq = kd[rows_, j % 2, a], qd[rows_, j % 2, a]

                                def score(out_, s, t):
                                    return pe.matmul(out_, kk[:, s], qq[:, t], start=True, stop=True)
                                for ch in range(2):
                                    o = ch * P
                                    if j < 6:
                                        last = score(ps[:, bank + 2 * ch + pr, a * P:(a + 1) * P],
                                                     slice(o, o + P), slice(o, o + P))
                                    elif j == 6:
                                        last = score(ps[0:64, bank + 2 * ch + pr, a * 64:(a + 1) * 64],
                                                     slice(o, o + 64), slice(o + 64, o + P))
                                    elif j == 7 and ch == 0:
                                        last = score(ps[:, bank + pr, a * P:(a + 1) * P], slice(0, P), slice(P, 2 * P))
                                    elif j == 8:
                                        at = (2 * ch + a) * TAIL
                                        last = score(ps[:, bank + pr, at:at + TAIL], slice(o, o + P), slice(2 * P, T))
                                if j < 4:
                                    at = 2 * P + a * TAIL
                                    last = score(ps[0:TAIL, bank + pr, at:at + TAIL], slice(2 * P, T), slice(2 * P, T))
                        last.then_inc(job_mm, 1)

                    pe.wait_ge(m_evac, 6 * m + 6)
                    job(0, 4)
                    pe.wait_ge(act_out, 4 * m + 1)
                    pe.wait_ge(pool_win, m + 1)
                    for a in range(2):
                        last = pe.matmul(ps[:, a, 0:T], wp[:, layer, a, :], y_tmp[:, a, :], start=True, stop=True)
                    last.then_inc(pool_mm, 1)
                    pe.wait_ge(cp_out, 6 * m + 1)
                    job(1, 4)
                    pe.wait_ge(y_ready, 8 * m + 4)
                    job(2, 0)
                    for j in (3, 4, 5, 6, 7):
                        pe.wait_ge(cp_out, 6 * m + j - 1)
                        job(j, 4 if j % 2 else 0)
                    pe.wait_ge(act_out, 4 * m + 2)
                    job(8, 0)
                    pe.wait_ge(act_out, 4 * m + 4)
                    for ch in range(3):
                        for hh in range(HEADS):
                            a, pr = hh // 2, hh % 2
                            n = P if ch < 2 else TAIL
                            parts = [(s_diag[:, 0, pr, a], 0)] if ch == 0 else \
                                [(s_next[:, hh, 0:P], 0), (s_diag[:, 1, pr, a], 1)] if ch == 1 else \
                                [(s_next[:, hh, P:P + TAIL], 0), (s_tail[:, hh], 1), (s_last[:, pr, a], 2)]
                            for n_, (sc, cs) in enumerate(parts):
                                vv = v_tok[:, cs] if cs < 2 else v_tok[0:TAIL, cs]
                                last = pe.matmul(ps[0:n, 4 + ch, hh * P:(hh + 1) * P], sc, vv[:, hh * P:(hh + 1) * P],
                                                 start=n_ == 0, stop=n_ == len(parts) - 1)
                    last.then_inc(o_mm, 1)

                    def out_unit(j, bank, per_k=None, **kw):
                        u = u0 + j
                        kh = 4 * ((j - 11) % 2)
                        unit(u % RING, u + 1 + RING, k_view(u % RING, 4, 512), range(kh, kh + 4), range(4),
                             bank, xs, t1, 0, KT - 1, per_k, **kw)
                    pe.wait_ge(y_lo, 8 * m + 4)
                    out_unit(11, 0)
                    pe.wait_ge(o_norm, m + 1)
                    for hh in range(HEADS):
                        for ch in range(2):
                            pe.transpose(ps[:, 4 + hh, ch * P:(ch + 1) * P], v_tok[:, ch, hh * P:(hh + 1) * P], ident)
                        last = pe.transpose(ps[:, 4 + hh, 2 * P:T], v_tok[0:TAIL, 2, hh * P:(hh + 1) * P],
                                            ident[0:TAIL, 0:TAIL])
                    last.then_inc(o_tr, 1)
                    y_tile = lambda kg: (y_lo, 8 * m + kg + 1)
                    out_unit(12, 0, y_tile)
                    out_unit(13, 4)
                    out_unit(14, 4, m_outer=True, half=half_done)
                    sum_f_most(bnd, t1)
                    sum_f_rest(bnd, t1)
            pe.wait_ge(h_ready, 8 * (NB + 1))
            for tt in range(2):
                for kk in range(KT):
                    last = pe.transpose(ps[:, 2 * tt + kk // 4, (kk % 4) * P:(kk % 4 + 1) * P],
                                        h[:, kk, NMETA + tt * P:NMETA + (tt + 1) * P], ident)
                last.then_inc(ends_tr, 1)


_INS = ["x", "meta", "ffn1_pre", "ffn1_post", "ffn1_wg", "ffn1_wu", "ffn1_wd", "mix_pre", "mix_post", "w_in",
        "pool_w", "pool_scale", "conv_w", "gla_w2", "gla_b2", "gla_norm", "w_out",
        "ffn2_pre", "ffn2_post", "ffn2_wg", "ffn2_wu", "ffn2_wd"]


def kernel(**inputs):
    import concourse.bacc as bacc
    from concourse.bass_utils import run_bass_kernel_spmd

    nc = bacc.Bacc("TRN2", target_bir_lowering=False, num_devices=1)
    arrays = {f"in_{n}": np.ascontiguousarray(inputs[n]) for n in _INS}
    arrays["in_consts"] = shape_constants(inputs["x"].shape[1] + NMETA)
    args = [nc.dram_tensor(n, a.shape, mybir.dt.from_np(a.dtype), kind="ExternalInput").ap()
            for n, a in arrays.items()]
    out = nc.dram_tensor("out", inputs["x"].shape, F32, kind="ExternalOutput").ap()
    trunk(nc, *args, out)
    r = run_bass_kernel_spmd(nc, [arrays], core_ids=[0])
    return r.results[0]["out"]
```

```python
from contextlib import ExitStack

import numpy as np
import concourse.bass as bass
from concourse import mybir

ALU = mybir.AluOpType
ACT = mybir.ActivationFunctionType
F32 = mybir.dt.float32
F32R = mybir.dt.float32r
I32 = mybir.dt.int32
U32 = mybir.dt.uint32

P = 128
NMETA = 16
D = 1024
KT = D // P
FF = 2816
FT = FF // P
GROUPS = FT // 2
HEADS = 4
EPS = 1e-6
RING = 4
UNIT = 2048
DOWN_K = (6, 6, 5, 5)
MAGIC = 1595932649.0
NEWTON = ((1.6819105, 0.70394764), (1.5000005, 0.50000016))
LOG_DECAY_MIN = -60.0
MIX_UNITS = 15
C_QK = 1024
PROJ = (("glow", 2048, 128), ("v0", 1536, 256), ("v1", 1792, 256), ("pool", 0, 256), ("cb", 256, 256),
        ("cc", 512, 256), ("cu", 768, 256), ("g0", 2064, 256), ("g1", 2320, 256))
OUT = {name: n + 1 for n, name in enumerate(("glow", "qk", "v0", "v1", "pool", "cb", "cc", "cu", "g0", "g1"))}
EVACS = len(OUT)
JOB_BANK = (4, 4, 4, 4, 0, 4, 0, 4, 0)
POOL_WINDOWS = (2, 4, 8, 16)
BASE = 2
LEVELS = (4, 8, 16, 32, 64)
JOBS = 9


def shape_constants(T):
    c = np.zeros((P, P + 2 * T + (1 + len(LEVELS)) * P), np.float32)
    c[:, 0:P] = np.eye(P)
    t = np.arange(T)
    for g, w in enumerate(POOL_WINDOWS):
        at = P + (g // 2) * T
        c[(g % 2) * 64:(g % 2) * 64 + 64, at:at + T] = 1.0 / np.minimum(t + 1, w)
    s, t = np.arange(P)[:, None], np.arange(P)[None, :]
    at = P + 2 * T
    c[:, at:at + P] = (s // BASE == t // BASE) & (s <= t)
    for n, bs in enumerate(LEVELS):
        at += P
        c[:, at:at + P] = (s // bs == t // bs) & (s % bs < bs // 2) & (t % bs >= bs // 2)
    return c


def trunk(nc, x, meta, ffn1_pre, ffn1_post, ffn1_wg, ffn1_wu, ffn1_wd, mix_pre, mix_post, w_in,
          pool_w, pool_scale, conv_w, gla_w2, gla_b2, gla_norm, w_out,
          ffn2_pre, ffn2_post, ffn2_wg, ffn2_wu, ffn2_wd, consts, out):
    SEQ = x.shape[1]
    T = SEQ + NMETA
    DEPTH = w_in.shape[0]
    TAIL = T - 2 * P

    FFN_UNITS = 2 * GROUPS + 4 * len(DOWN_K)
    phases = []
    u0 = 0
    for layer in range(DEPTH):
        for kind in ("ffn1", "mix", "ffn2"):
            last = layer == DEPTH - 1
            phases.append(dict(
                kind=kind, layer=layer, u0=u0, b=len(phases),
                f=2 * layer + (kind == "ffn2"),
                m=layer,
                t_in=NMETA if last and kind == "ffn2" else 0,
                t_out=NMETA if last and kind != "ffn1" else 0))
            u0 += MIX_UNITS if kind == "mix" else FFN_UNITS
    NB = len(phases)

    def weights(ph):
        wg, wu, wd = (ffn1_wg, ffn1_wu, ffn1_wd) if ph["kind"] == "ffn1" else (ffn2_wg, ffn2_wu, ffn2_wd)
        tiled = lambda w: w[ph["layer"]].rearrange("(k p) n -> p k n", p=P)
        return tiled(wg), tiled(wu), tiled(wd)

    ctx = ExitStack()
    with ctx:
        def sb(name, shape, dt=F32):
            return ctx.enter_context(nc.sbuf_tensor(name, shape, dt))

        def sem(name):
            return ctx.enter_context(nc.semaphore(name))

        h = sb("h", [P, KT, T])
        x_hi = sb("x_hi", [P, KT, T], F32R)
        x_lo = sb("x_lo", [P, KT, T], F32R)
        f = sb("f", [P, KT, T])
        raw = sb("raw", [P, RING, UNIT])
        w_hi = sb("w_hi", [P, RING, UNIT], F32R)
        w_lo = sb("w_lo", [P, RING, UNIT], F32R)
        cst = sb("cst", [P, P + 2 * T + (1 + len(LEVELS)) * P])
        ones = sb("ones", [P, T])
        par = sb("par", [P, P])
        r_post = sb("r_post", [P, T])
        r_pre = sb("r_pre", [P, T])
        ms = sb("ms", [P, T])
        nt = sb("nt", [P, T])
        w2 = sb("w2", [NMETA, DEPTH, 256])
        wp = sb("wp", [P, DEPTH, 2, P])
        ident = cst[:, 0:P]
        inv_count = cst[:, P:P + 2 * T].rearrange("p (a t) -> p a t", a=2)
        sq_acc = sb("sq_acc", [P, 2, T])
        sq_new = sb("sq_new", [P, 2, T])
        pre_acc = sb("pre_acc", [P, 2, T])
        small = sb("small", [P, 4, 12])

        def mask(n, rows):
            at = P + 2 * T + n * P
            return cst[0:rows, at:at + rows].bitcast(U32)

        ffn_floats = 2 * FT * T + 8 * T
        PAD = 16
        mix_floats = (5 * 2 + 4 + 3 * 4 + 4 + 4) * T + 1536 + 1024 + 4 * (P + TAIL) + 4 * TAIL \
            + 4 * TAIL + 2 * (2 + T)
        arena_bytes = 4 * max(ffn_floats, mix_floats)
        arena = sb("arena", [P, arena_bytes // 4])
        arena_at = nc.sbuf_base - arena_bytes
        laid = [0]

        def place(name, shape, dt=F32):
            n = 4 * int(np.prod(shape[1:]))
            t = nc.alloc_sbuf_tensor_at(name, shape, dt, offset=arena_at + laid[0])
            laid[0] += n
            assert laid[0] <= arena_bytes, (name, laid[0], arena_bytes)
            return t

        hid_hi = place("hid_hi", [P, FT, T], F32R)
        hid_lo = place("hid_lo", [P, FT, T], F32R)
        gate = place("gate", [P, 2, 2, T])
        up = place("up", [P, 2, 2, T])
        laid[0] = 0
        x_tok = place("x_tok", [P, 2, D])
        meta_tok = place("meta_tok", [NMETA, D])
        par_rows = place("par_rows", [P, P])
        out_tok = place("out_tok", [P, 2, D])
        laid[0] = 0
        q = place("q", [P, 2, T])
        k = place("k", [P, 2, T])
        v = place("v", [P, 4, T])
        b = place("b", [P, 2, T])
        la = place("la", [P, 2, T])
        lt = place("lt", [P, 2, T])
        dec = place("dec", [P, 2, 2, T])
        qd = place("qd", [P, 2, 2, T])
        kd = place("kd", [P, 2, 2, T])
        v_tok = place("v_tok", [P, 3, 512])
        s_diag = place("s_diag", [P, 2, 2, 2, P])
        s_next = place("s_next", [P, 4, P + TAIL])
        s_tail = place("s_tail", [P, 4, TAIL])
        s_last = place("s_last", [TAIL, 2, 2, TAIL])
        g_out = place("g_out", [P, 4, T])
        c_cu = place("c_cu", [P, 4, T])
        z_pad = place("z_pad", [P, 2, 2 + T])
        glow = z_pad[0:NMETA, 0, 2:2 + T]
        y_tmp = la
        inv_dec = lt
        c_b = lt
        y_head = v
        f_flat = f[:, :, :].rearrange("p k t -> p (k t)")
        n_win = 2 * (PAD + T)
        pool_in, win_a, win_b = (f_flat[:, i * n_win:(i + 1) * n_win].rearrange("p (a t) -> p a t", a=2)
                                 for i in range(3))

        ps = ctx.enter_context(nc.psum_tensor("ps", [P, 8, 512], F32))

        raw_in = [sem(f"raw_in{i}") for i in range(RING)]
        unit_hi = sem("unit_hi")
        unit_lo = sem("unit_lo")
        unit_used = sem("unit_used")
        par_in = sem("par_in")
        mix_in = sem("mix_in")
        x_in = sem("x_in")
        zeroed = sem("zeroed")
        ones_set = sem("ones_set")
        ends_tr = sem("ends_tr")
        staged = [sem(f"staged{i}") for i in range(4)]
        par_ready = sem("par_ready")
        h_ready = sem("h_ready")
        xh_ready = sem("xh_ready")
        xl_ready = sem("xl_ready")
        sq_ready = sem("sq_ready")
        pre_sum = sem("pre_sum")
        ss_pre = sem("ss_pre")
        ms_read = sem("ms_read")
        rpre_ready = sem("rpre_ready")
        dve = sem("dve")
        gate_ready = sem("gate_ready")
        silu_done = sem("silu_done")
        up_evac = sem("up_evac")
        hid_mul = sem("hid_mul")
        hid_hi_ready = sem("hid_hi_ready")
        hid_lo_ready = sem("hid_lo_ready")
        pair_out = sem("pair_out")
        sq_pair = sem("sq_pair")
        sq_sum = sem("sq_sum")
        ss_post = sem("ss_post")
        done_out = sem("done_out")
        m_evac = sem("m_evac")
        m_cleared = sem("m_cleared")
        half_done = sem("half_done")
        tile_done = sem("tile_done")
        z_mm = sem("z_mm")
        z_out = sem("z_out")
        lt_step = sem("lt_step")
        dec_arg = sem("dec_arg")
        dec_exp = sem("dec_exp")
        qk_dec = sem("qk_dec")
        job_mm = sem("job_mm")
        vt_mm = sem("vt_mm")
        act_out = sem("act_out")
        act_cp = sem("act_cp")
        cp_out = sem("cp_out")
        g_silu = sem("g_silu")
        pool_win = sem("pool_win")
        pool_own = sem("pool_own")
        pool_mm = sem("pool_mm")
        pool_out = sem("pool_out")
        y_ready = sem("y_ready")
        y_hi = sem("y_hi")
        y_lo = sem("y_lo")
        o_mm = sem("o_mm")
        o_sq = sem("o_sq")
        o_norm = sem("o_norm")
        o_tr = sem("o_tr")

        block = ctx.enter_context(nc.Block())

        C = {}
        rows = [("ffn1_pre", ffn1_pre, KT), ("ffn1_post", ffn1_post, KT), ("mix_pre", mix_pre, KT),
                ("mix_post", mix_post, KT), ("ffn2_pre", ffn2_pre, KT), ("ffn2_post", ffn2_post, KT),
                ("pool_scale", pool_scale, 2), ("conv_w", conv_w, 6), ("gla_b2", gla_b2, 2),
                ("gla_norm", gla_norm, 4)]
        n_rows = 0
        for name, _, per in rows:
            C[name] = (n_rows, per)
            n_rows += DEPTH * per

        def col(name, layer, i):
            base, per = C[name]
            c = base + layer * per + i
            return par[:, c:c + 1]

        def f32(ap):
            return ap.bitcast(F32)

        def sum_bank(ph):
            return 5 if ph["kind"] == "mix" else 4

        def last_of(ph, what):
            return ph["u0"] + what + 1 + RING

        UP_UNITS = 2 * GROUPS
        MIX_SIZE = [UNIT] * 2 + [1024] + [UNIT] * 12

        @block.sync
        def _(sp):
            def load(slot, value, *copies):
                sp.wait_ge(unit_lo, value)
                for dst, src in copies:
                    sp.dma_start(dst, src).then_inc(raw_in[slot], 16)

            sp.dma_start(meta_tok[:, :], meta).then_inc(x_in, 16)
            for tt in range(2):
                sp.dma_start(x_tok[:, tt], x[0, tt * P:(tt + 1) * P, :]).then_inc(x_in, 16)
            for ph in phases:
                u0, layer = ph["u0"], ph["layer"]
                if ph["kind"] != "mix":
                    wg, wu, wd = weights(ph)

                    def up_unit(j, value, cols):
                        slot = (u0 + j) % RING
                        dst = raw[:, slot].rearrange("p (s k n) -> p s k n", s=2, k=4)
                        ks = slice(4 * (j % 2), 4 * (j % 2) + 4)
                        load(slot, value, (dst[:, 0], wg[:, ks, cols]), (dst[:, 1], wu[:, ks, cols]))

                    for j in range(2):
                        up_unit(j, u0 + j + 1, slice(0, 256))
                    with sp.Fori(0, GROUPS // 2) as i:
                        for j in range(4):
                            up_unit(2 + j, i * 4 + (u0 + 2 + j + 1), bass.ds(i * 512 + 256 + 256 * (j // 2), 256))
                    with sp.Fori(0, KT // 2) as i:
                        k0 = 0
                        for j, nk in enumerate(DOWN_K):
                            slot = (u0 + UP_UNITS + j) % RING
                            dst = raw[:, slot, 0:nk * 256].rearrange("p (k n) -> p k n", k=nk)
                            cols = bass.ds(i * 256, 256)
                            load(slot, i * 4 + (u0 + UP_UNITS + j + 1),
                                 (dst[:, 0:3], wd[:, k0:k0 + 3, cols]), (dst[:, 3:nk], wd[:, k0 + 3:k0 + nk, cols]))
                            k0 += nk
                else:
                    wi = w_in[layer].rearrange("(k p) n -> p k n", p=P)
                    wo = w_out[layer].rearrange("(k p) n -> p k n", p=P)

                    def block_unit(j, w, k0, nk, c0, n):
                        slot = (u0 + j) % RING
                        dst = raw[:, slot, 0:nk * n].rearrange("p (k n) -> p k n", k=nk)
                        half = nk // 2
                        load(slot, u0 + j + 1, (dst[:, 0:half], w[:, k0:k0 + half, c0:c0 + n]),
                             (dst[:, half:nk], w[:, k0 + half:k0 + nk, c0:c0 + n]))
                    block_unit(0, wi, 0, 4, C_QK, 512)
                    block_unit(1, wi, 4, 4, C_QK, 512)
                    for j, (_, c0, n) in enumerate(PROJ):
                        block_unit(2 + j, wi, 0, 8, c0, n)
                    for j in range(4):
                        block_unit(11 + j, wo, 4 * (j % 2), 4, 512 * (j // 2), 512)
            for n, (half, tt) in enumerate(((0, 0), (0, 1), (1, 0), (1, 1))):
                cols = slice(half * 512, half * 512 + 512)
                sp.wait_ge(staged[n], 1)
                sp.dma_start(out[0, tt * P:(tt + 1) * P, cols], out_tok[:, tt, cols]).then_inc(done_out, 16)
            sp.wait_ge(done_out, 64)

        @block.scalar
        def _(act):
            act.dma_start(cst[:, :], consts).then_inc(par_in, 16)
            for name, src, per in rows:
                r0 = C[name][0]
                if name == "conv_w":
                    by_tile = src.rearrange("l j (a p) -> (l j a) p", p=P)
                else:
                    by_tile = src.rearrange("l (a p) -> (l a) p", p=P)
                act.dma_start(par_rows[r0:r0 + DEPTH * per, :], by_tile).then_inc(par_in, 16)
            act.dma_start(w2[:, :, :], gla_w2.rearrange("l r n -> r l n")).then_inc(mix_in, 16)
            act.wait_ge(zeroed, 1)
            for g in range(2):
                act.dma_start(wp[g * 64:g * 64 + 64, :, :, g * 64:g * 64 + 64].rearrange("c l a d -> c (l a) d"),
                              pool_w.rearrange("l (a g) c d -> g c (l a) d", g=2)[g]).then_inc(mix_in, 16)

            def high(slot, n, arrived, free):
                act.wait_ge(raw_in[slot], arrived)
                act.wait_ge(unit_used, free)
                act.activation(w_hi[:, slot, 0:n], raw[:, slot, 0:n], ACT.Copy).then_inc(unit_hi, 1)

            def high_unit(u, n):
                high(u % RING, n, 32 * (u // RING + 1), u + 1)

            def split_h(bnd, gain, layer, t0):
                for kk in range(KT):
                    act.wait_ge(h_ready, 8 * bnd + kk + 1)
                    act.activation(x_hi[:, kk, t0:T], h[:, kk, t0:T], ACT.Copy,
                                   scale=col(gain, layer, kk)).then_inc(xh_ready, 1)
                    act.activation(f[:, kk, t0:T], h[:, kk, t0:T], ACT.Square).then_inc(sq_ready, 1)

            def pair_evac(blk, pair, bank, t0, sem_, count):
                src = ps[:, bank:bank + 2, 0:T - t0]
                if pair < 3:
                    act.wait_ge(sem_, count)
                    if pair == 2:
                        act.wait_ge(sq_sum, 3 * blk + 1)
                    dst = sq_acc if pair == 0 else sq_new
                    act.activation(dst[:, :, t0:T], src, ACT.Square).then_inc(sq_pair, 1)
                else:
                    act.wait_ge(sq_sum, 3 * blk + 2)
                    act.wait_ge(tile_done, blk + 1)
                    act.activation(sq_new[:, 0, t0:T], src[:, 0], ACT.Square).then_inc(sq_pair, 1)
                    act.wait_ge(sem_, count)
                    act.activation(sq_new[:, 1, t0:T], src[:, 1], ACT.Square).then_inc(sq_pair, 1)
                act.activation(f[:, 2 * pair:2 * pair + 2, t0:T], src, ACT.Copy).then_inc(pair_out, 1)

            high_unit(0, UNIT)
            act.wait_ge(par_ready, 1)
            for ph in phases:
                u0, layer, bnd, t0 = ph["u0"], ph["layer"], ph["b"], ph["t_in"]
                split_h(bnd, {"ffn1": "ffn1_pre", "mix": "mix_pre", "ffn2": "ffn2_pre"}[ph["kind"]], layer, t0)
                for u in range(3 if bnd else 1, RING):
                    high_unit(u0 + u, UNIT)
                if ph["kind"] != "mix":
                    fi = ph["f"]

                    def group(parity, ua, i4, i32, idx, dst):
                        high(ua % RING, UNIT, i32 + 32 * (ua // RING + 1), i4 + (ua + 1))
                        act.wait_ge(gate_ready, idx)
                        act.activation(gate[:, parity, :, t0:T], gate[:, parity, :, t0:T], ACT.Silu)\
                           .then_inc(silu_done, 1)
                        high((ua + 1) % RING, UNIT, i32 + 32 * ((ua + 1) // RING + 1), i4 + (ua + 2))
                        act.wait_ge(hid_mul, idx)
                        act.activation(dst, up[:, parity, :, t0:T], ACT.Copy).then_inc(hid_hi_ready, 1)

                    group(0, u0 + RING, 0, 0, GROUPS * fi + 1, hid_hi[:, 0:2, t0:T])
                    with act.Fori(0, GROUPS // 2) as i:
                        for g in (1, 2):
                            group(g % 2, u0 + 2 * g + RING, i * 4, i * 32, i * 2 + (GROUPS * fi + g + 1),
                                  hid_hi[:, bass.ds(i * 4 + 2 * g, 2), t0:T])
                    d0 = u0 + UP_UNITS
                    for pair in range(KT // 2):
                        last_pair = pair == KT // 2 - 1
                        for j in range(4):
                            u = d0 + 4 * pair + j + RING
                            if not last_pair:
                                high_unit(u, DOWN_K[j] * 256)
                            elif j < 3 and bnd < NB - 1:
                                high_unit(u, UNIT)
                        pair_evac(bnd, pair, 4 + 2 * (pair % 2), t0, unit_used, last_of(ph, UP_UNITS + 4 * pair + 3))
                else:
                    m, t1 = ph["m"], ph["t_out"]

                    def ahead(j):
                        high_unit(u0 + j + RING, MIX_SIZE[j + RING] if j + RING < MIX_UNITS else UNIT)

                    def decays(j):
                        act.wait_ge(dec_arg, JOBS * m + j + 1)
                        n = T if j < 4 or j == JOBS - 1 else 2 * P
                        if j == 0:
                            act.activation(inv_dec[:, :, :], dec[:, 0], ACT.Exp, scale=-1.0).then_inc(act_cp, 1)
                            act.wait_ge(act_cp, m + 1)
                        act.activation(dec[:, j % 2, :, 0:n], dec[:, j % 2, :, 0:n], ACT.Exp).then_inc(dec_exp, 1)

                    for j in range(4):
                        ahead(j)
                    act.wait_ge(z_out, m + 1)
                    act.activation(lt[:, :, :], la[:, :, :], ACT.Abs).then_inc(lt_step, 1)
                    act.wait_ge(lt_step, 3 * m + 1)
                    act.activation(lt[:, :, :], lt[:, :, :], ACT.Exp, scale=-1.0).then_inc(lt_step, 1)
                    act.wait_ge(lt_step, 3 * m + 2)
                    act.activation(lt[:, :, :], lt[:, :, :], ACT.Ln, bias=1.0).then_inc(lt_step, 1)
                    ahead(4)
                    decays(0)
                    decays(1)
                    ahead(5)
                    act.wait_ge(vt_mm, m + 1)
                    act.activation(v_tok[:, 0:2, :], ps[:, 4:6, :], ACT.Copy)
                    act.activation(v_tok[0:TAIL, 2, :], ps[0:TAIL, 6, :], ACT.Copy).then_inc(act_out, 1)
                    decays(2)
                    ahead(6)
                    decays(3)
                    decays(4)
                    ahead(7)
                    decays(5)
                    ahead(8)
                    decays(6)
                    decays(7)
                    decays(8)
                    act.wait_ge(cp_out, 6 * m + 6)
                    act.wait_ge(job_mm, JOBS * m + 7)
                    for c in range(2):
                        src = ps[0:64, 2 * c:2 * c + 2, 0:P].rearrange("p b (a t) -> p b a t", a=2)
                        last = act.activation(s_diag[0:64, c, :, :, 64:P], src, ACT.Copy)
                    last.then_inc(act_out, 1)
                    act.wait_ge(job_mm, JOBS * m + 8)
                    for pr in range(2):
                        last = act.activation(s_next[:, pr:4:2, 0:P],
                                              ps[:, 4 + pr, 0:2 * P].rearrange("p (a t) -> p a t", a=2), ACT.Copy)
                    last.then_inc(act_out, 1)
                    act.wait_ge(job_mm, JOBS * m + 9)
                    for pr in range(2):
                        both = ps[:, pr, 0:4 * TAIL].rearrange("p (c a t) -> p c a t", c=2, a=2)
                        act.activation(s_next[:, pr:4:2, P:P + TAIL], both[:, 0], ACT.Copy)
                        last = act.activation(s_tail[:, pr:4:2, :], both[:, 1], ACT.Copy)
                    last.then_inc(act_out, 1)
                    act.wait_ge(o_mm, m + 1)
                    sq_o = qd[:, :, :, :].rearrange("p a b t -> p (a b t)")
                    act.activation(sq_o[:, 0:1024].rearrange("p (c n) -> p c n", c=2), ps[:, 4:6, :], ACT.Square)
                    act.activation(kd[:, :, :, :].rearrange("p a b t -> p (a b t)")[0:TAIL, 0:512], ps[0:TAIL, 6, :],
                                   ACT.Square).then_inc(o_sq, 1)
                    ahead(9)
                    act.wait_ge(unit_used, last_of(ph, 10))

                    def high_y(n, kk, src):
                        act.wait_ge(y_ready, 8 * m + n)
                        act.activation(x_hi[:, kk, :], src, ACT.Copy).then_inc(y_hi, 1)
                    for kk in range(4):
                        high_y(4, kk, (y_tmp if kk < 2 else c_cu)[:, kk % 2, :])
                    act.wait_ge(m_evac, EVACS * m + OUT["g1"])
                    act.activation(g_out[:, :, :], g_out[:, :, :], ACT.Silu).then_inc(g_silu, 1)
                    for a in range(4):
                        high_y(a + 5, 4 + a, y_head[:, a, :])
                    ahead(10)
                    ahead(11)
                    ahead(12)
                    for pair in range(2):
                        pair_evac(bnd, pair, 2 * pair, t1, unit_used, last_of(ph, 12))
                    ahead(13)
                    pair_evac(bnd, 2, 4, t1, half_done, m + 1)
                    pair_evac(bnd, 3, 6, t1, unit_used, last_of(ph, 14))
            for n, bank in enumerate((0, 2, 1)):
                act.wait_ge(ends_tr, 3 + n)
                act.activation(out_tok[:, bank // 2, (bank % 2) * 512:(bank % 2 + 1) * 512], ps[:, bank, :], ACT.Copy)\
                   .then_inc(staged[n], 1)

        @block.vector
        def _(v_):
            own = [0]

            def mark(ins):
                ins.then_inc(dve, 1)
                own[0] += 1
                return own[0]

            def low(slot, n, count):
                v_.wait_ge(unit_hi, count)
                v_.tensor_tensor(w_lo[:, slot, 0:n], raw[:, slot, 0:n], f32(w_hi[:, slot, 0:n]), ALU.subtract)\
                  .then_inc(unit_lo, 1)

            def low_unit(u, n):
                low(u % RING, n, u + 1)

            def rsqrt(src, n, mean, tmp, dst, read=None):
                ins = v_.tensor_scalar(mean, src, 1.0 / n, EPS, ALU.mult, ALU.add)
                c = mark(ins)
                v_.wait_ge(dve, c)
                if read is not None:
                    v_.sem_inc(read, 1)
                c = mark(v_.tensor_scalar(dst.bitcast(I32), mean.bitcast(I32), -0.5, MAGIC, ALU.mult, ALU.add))
                for plus, minus in NEWTON:
                    v_.wait_ge(dve, c)
                    c = mark(v_.tensor_tensor(tmp, dst, dst, ALU.mult))
                    v_.wait_ge(dve, c)
                    c = mark(v_.scalar_tensor_tensor(tmp, tmp, -minus, mean, ALU.mult, ALU.mult))
                    v_.wait_ge(dve, c)
                    c = mark(v_.scalar_tensor_tensor(dst, tmp, plus, dst, ALU.add, ALU.mult))
                v_.wait_ge(dve, c)

            def tok(r, a, t0):
                return r[:, t0:T].unsqueeze(1).to_broadcast([P, a, T - t0])

            def new_h(bnd, post, pre, layer, layer_pre, t0, final):
                def low_x(kk):
                    v_.wait_ge(xh_ready, 8 * bnd + kk + 1)
                    v_.scalar_tensor_tensor(x_lo[:, kk, t0:T], h[:, kk, t0:T], col(pre, layer_pre, kk),
                                            f32(x_hi[:, kk, t0:T]), ALU.mult, ALU.subtract).then_inc(xl_ready, 1)
                c = {}

                def scale(kk, n):
                    v_.wait_ge(pair_out, 4 * (bnd - 1) + kk // 2 + 1)
                    c[kk] = c[kk + n - 1] = mark(v_.tensor_tensor(
                        f[:, kk:kk + n, t0:T], f[:, kk:kk + n, t0:T], tok(r_post, n, t0), ALU.mult))

                def add(kk):
                    v_.wait_ge(dve, c[kk])
                    v_.scalar_tensor_tensor(h[:, kk, t0:T], f[:, kk, t0:T], col(post, layer, kk),
                                            h[:, kk, t0:T], ALU.mult, ALU.add).then_inc(h_ready, 1)
                scale(0, 1)
                scale(1, 1)
                add(0)
                for kk in range(1, KT):
                    if kk % 2 and kk + 1 < KT:
                        scale(kk + 1, 2)
                    add(kk)
                    if kk > 1 and not final:
                        low_x(kk - 2)
                if not final:
                    low_x(KT - 2)
                    low_x(KT - 1)

            v_.memset(ones[:, :], 1.0).then_inc(ones_set, 1)
            for _ in range(RING):
                v_.sem_inc(unit_lo, 1)
            v_.sem_inc(up_evac, 1)
            v_.sem_inc(up_evac, 1)
            v_.wait_ge(ends_tr, 1)
            c = mark(v_.tensor_copy(par[:, 0:n_rows], ps[:, 7, T:T + n_rows]))
            v_.wait_ge(dve, c)
            for name in ("ffn1_post", "ffn2_post"):
                cs = slice(C[name][0], C[name][0] + DEPTH * KT)
                c = mark(v_.tensor_scalar(par[:, cs], par[:, cs], 0.5, None, ALU.mult))
            v_.wait_ge(dve, c)
            v_.sem_inc(par_ready, 1)
            v_.wait_ge(ends_tr, 2)
            for kk in range(KT):
                v_.tensor_copy(h[:, kk, :], ps[:, kk, 0:T]).then_inc(h_ready, 1)
            low_unit(0, UNIT)
            for kk in range(KT):
                v_.wait_ge(xh_ready, kk + 1)
                v_.scalar_tensor_tensor(x_lo[:, kk, :], h[:, kk, :], col("ffn1_pre", 0, kk),
                                        f32(x_hi[:, kk, :]), ALU.mult, ALU.subtract).then_inc(xl_ready, 1)
            POST = {"ffn1": "ffn1_post", "mix": "mix_post", "ffn2": "ffn2_post"}
            PRE = {"ffn1": "ffn1_pre", "mix": "mix_pre", "ffn2": "ffn2_pre"}
            for ph in phases:
                u0, layer, bnd, t0 = ph["u0"], ph["layer"], ph["b"], ph["t_in"]
                for u in range(3 if bnd else 1, RING):
                    low_unit(u0 + u, UNIT)

                def pre_rms():
                    v_.wait_ge(ss_pre, bnd + 1)
                    rsqrt(ps[:, sum_bank(ph), 0:T - t0], D, ms[:, t0:T], nt[:, t0:T], r_pre[:, t0:T], read=ms_read)

                def sum_squares(pair, ts):
                    v_.wait_ge(sq_pair, 5 * bnd + pair + 1)
                    v_.tensor_tensor(sq_acc[:, :, ts:T], sq_acc[:, :, ts:T], sq_new[:, :, ts:T], ALU.add)\
                      .then_inc(sq_sum, 1)
                    if pair == 2:
                        v_.wait_ge(sq_sum, 3 * bnd + 2)
                        v_.tensor_tensor(sq_acc[:, 0, ts:T], sq_acc[:, 0, ts:T], sq_acc[:, 1, ts:T], ALU.add)\
                          .then_inc(sq_sum, 1)

                if ph["kind"] != "mix":
                    fi = ph["f"]

                    def group(parity, ua, i4, idx):
                        low(ua % RING, UNIT, i4 + (ua + 1))
                        v_.wait_ge(unit_used, i4 + (ua + 2))
                        v_.wait_ge(hid_lo_ready, idx)
                        bank = 4 * parity
                        v_.tensor_tensor(gate[:, parity, :, t0:T], ps[:, bank:bank + 2, 0:T - t0],
                                         tok(r_pre, 2, t0), ALU.mult).then_inc(gate_ready, 1)
                        v_.tensor_tensor(up[:, parity, :, t0:T], ps[:, bank + 2:bank + 4, 0:T - t0],
                                         tok(r_pre, 2, t0), ALU.mult).then_inc(up_evac, 1)
                        low((ua + 1) % RING, UNIT, i4 + (ua + 2))

                    pre_rms()
                    group(0, u0 + RING, 0, GROUPS * fi + 1)
                    with v_.Fori(0, GROUPS // 2) as i:
                        for g in (1, 2):
                            group(g % 2, u0 + 2 * g + RING, i * 4, i * 2 + (GROUPS * fi + g + 1))
                    d0 = u0 + UP_UNITS
                    for pair in range(KT // 2):
                        last_pair = pair == KT // 2 - 1
                        for j in range(4):
                            u = d0 + 4 * pair + j + RING
                            if not last_pair:
                                low_unit(u, DOWN_K[j] * 256)
                            elif j < 3 and bnd < NB - 1:
                                low_unit(u, UNIT)
                        if pair in (1, 2):
                            sum_squares(pair, t0)
                    t_end = t0
                else:
                    m, t_end = ph["m"], ph["t_out"]

                    def ahead(j):
                        low_unit(u0 + j + RING, MIX_SIZE[j + RING] if j + RING < MIX_UNITS else UNIT)

                    def by_block(x_, bs, n):
                        return x_[:, :, 0:n].rearrange("p a (n s) -> p a n s", s=bs)

                    def exponents(j):
                        if j >= 2:
                            v_.wait_ge(qk_dec, JOBS * m + j - 1)
                        d = dec[:, j % 2]
                        if j == 0:
                            bb = by_block(b, BASE, T)
                            ref = bb[:, :, :, 0:1].to_broadcast([P, 2, T // BASE, BASE])
                            v_.tensor_tensor(by_block(d, BASE, T), bb, ref, ALU.subtract).then_inc(dec_arg, 1)
                        elif j < JOBS - 1:
                            bs = 2 * BASE << (j - 1)
                            n = T if T % bs == 0 else 2 * P
                            bb, dd, hf = by_block(b, bs, n), by_block(d, bs, n), bs // 2
                            ref = bb[:, :, :, hf - 1:hf].to_broadcast([P, 2, n // bs, hf])
                            v_.tensor_tensor(dd[:, :, :, 0:hf], ref, bb[:, :, :, 0:hf], ALU.subtract)
                            v_.tensor_tensor(dd[:, :, :, hf:bs], bb[:, :, :, hf:bs], ref, ALU.subtract)\
                              .then_inc(dec_arg, 1)
                        else:
                            ref = b[:, :, 2 * P - 1:2 * P]
                            v_.tensor_tensor(d[:, :, 0:2 * P], ref.to_broadcast([P, 2, 2 * P]), b[:, :, 0:2 * P],
                                             ALU.subtract)
                            v_.tensor_tensor(d[:, :, 2 * P:T], b[:, :, 2 * P:T], ref.to_broadcast([P, 2, TAIL]),
                                             ALU.subtract).then_inc(dec_arg, 1)

                    def take_scores(j):
                        v_.wait_ge(job_mm, JOBS * m + j + 1)
                        v_.wait_ge(m_cleared, m + 1)
                        bank = JOB_BANK[j]
                        src = ps[:, bank:bank + 4, 0:2 * P].rearrange("p b (a t) -> p b a t", a=2)
                        dst = s_diag[:, :, :, :, :].rearrange("p c b a t -> p (c b) a t")
                        if j:
                            v_.wait_ge(cp_out, 6 * m + j)
                        last = v_.copy_predicated(dst, mask(j, P).unsqueeze(1).unsqueeze(1).to_broadcast([P, 4, 2, P]), src)
                        if j < 4:
                            last = v_.copy_predicated(
                                s_last[:, :, :, :],
                                mask(j, TAIL).unsqueeze(1).unsqueeze(1).to_broadcast([TAIL, 2, 2, TAIL]),
                                ps[0:TAIL, bank:bank + 2, 2 * P:2 * P + 2 * TAIL].rearrange("p b (a t) -> p b a t", a=2))
                        last.then_inc(cp_out, 1)

                    def low_y(n, kk, src):
                        v_.wait_ge(y_hi, 8 * m + n)
                        v_.tensor_tensor(x_lo[:, kk, :], src, f32(x_hi[:, kk, :]), ALU.subtract).then_inc(y_lo, 1)

                    def out_of_psum(name, dst, bank, n_tiles=2, used=None):
                        if used is not None:
                            v_.wait_ge(unit_used, last_of(ph, used))
                        ins = v_.tensor_tensor(dst, ps[:, bank:bank + n_tiles, 0:T], tok(r_pre, n_tiles, 0), ALU.mult)
                        ins.then_inc(m_evac, 1)

                    ahead(0)
                    ahead(1)
                    pre_rms()
                    v_.wait_ge(unit_used, last_of(ph, 2))
                    v_.tensor_tensor(glow, ps[0:NMETA, 4, 0:T], r_pre[0:NMETA, :], ALU.mult).then_inc(m_evac, 1)
                    v_.scalar_tensor_tensor(q[:, :, :], ps[:, 0:2, 0:T], 0.125, tok(r_pre, 2, 0), ALU.mult, ALU.mult)
                    out_of_psum("qk", k[:, :, :], 2)
                    ahead(2)
                    ahead(3)
                    out_of_psum("v0", v[:, 0:2, :], 6)
                    v_.wait_ge(z_mm, m + 1)
                    for a in range(2):
                        last = v_.tensor_scalar(la[:, a, :], ps[:, a, 0:T], col("gla_b2", layer, a), None, ALU.add)
                    last.then_inc(z_out, 1)
                    v_.wait_ge(lt_step, 3 * m + 3)
                    flat = lambda x_: x_[:, :, :].rearrange("p a t -> p (a t)")
                    c = mark(v_.scalar_tensor_tensor(flat(la), flat(la), 0.0, flat(lt), ALU.min, ALU.subtract))
                    v_.wait_ge(dve, c)
                    c = mark(v_.tensor_scalar(flat(la), flat(la), 1.0 / 16, LOG_DECAY_MIN, ALU.mult, ALU.max))
                    v_.wait_ge(dve, c)
                    for a in range(2):
                        c = mark(v_.tensor_tensor_scan(b[:, a, :], ones[:, 0:T], la[:, a, :], 0.0, ALU.mult, ALU.add))
                    v_.wait_ge(dve, c)
                    exponents(0)
                    exponents(1)
                    ahead(4)
                    out_of_psum("v1", v[:, 2:4, :], 4, used=4)
                    ahead(5)
                    v_.wait_ge(m_cleared, m + 1)
                    out_of_psum("pool", pool_in[:, :, PAD:PAD + T], 2, used=5)
                    exponents(2)
                    ahead(6)
                    out_of_psum("cb", c_b[:, :, :], 0, used=6)
                    exponents(3)
                    take_scores(0)
                    exponents(4)
                    ahead(7)
                    out_of_psum("cc", c_cu[:, 0:2, :], 2, used=7)
                    take_scores(1)
                    exponents(5)
                    ahead(8)
                    out_of_psum("cu", c_cu[:, 2:4, :], 0, used=8)
                    take_scores(2)
                    exponents(6)
                    v_.wait_ge(m_evac, EVACS * m + OUT["cu"])
                    c = mark(v_.tensor_tensor(z_pad[:, :, 2:2 + T], c_cu[:, 0:2, :], c_cu[:, 2:4, :], ALU.mult))
                    v_.wait_ge(dve, c)
                    for a in range(2):
                        c = mark(v_.tensor_scalar(c_cu[:, a, :], z_pad[:, a, 2:2 + T], col("conv_w", layer, 4 + a),
                                                  None, ALU.mult))
                    for j in (1, 0):
                        for a in range(2):
                            v_.wait_ge(dve, c - 1)
                            c = mark(v_.scalar_tensor_tensor(c_cu[:, a, :], z_pad[:, a, j:j + T],
                                                             col("conv_w", layer, 2 * j + a), c_cu[:, a, :],
                                                             ALU.mult, ALU.add))
                    for a in range(2):
                        v_.wait_ge(dve, c - 1 + a)
                        v_.tensor_tensor(c_cu[:, a, :], c_cu[:, a, :], c_b[:, a, :], ALU.mult).then_inc(y_ready, 1)
                    v_.wait_ge(pool_mm, m + 1)
                    for a in range(2):
                        v_.tensor_scalar(y_tmp[:, a, :], ps[:, 2 + a, 0:T], col("pool_scale", layer, a), None, ALU.mult)\
                          .then_inc(y_ready, 1)
                    take_scores(3)
                    exponents(7)
                    take_scores(4)
                    exponents(8)
                    take_scores(5)
                    v_.wait_ge(o_sq, m + 1)
                    sq_o = qd[:, :, :, :].rearrange("p a b t -> p (a b t)")
                    v_.tensor_reduce(small[:, 0, 0:8], sq_o[:, 0:1024].rearrange("p (a n) -> p a n", a=8),
                                     mybir.AxisListType.X, ALU.add)
                    c = mark(v_.tensor_reduce(
                        small[0:TAIL, 0, 8:12],
                        kd[:, :, :, :].rearrange("p a b t -> p (a b t)")[0:TAIL, 0:512].rearrange("p (a n) -> p a n", a=4),
                        mybir.AxisListType.X, ALU.add))
                    v_.wait_ge(dve, c)
                    rsqrt(small[:, 0], P, small[:, 1], small[:, 2], small[:, 3])
                    for ch in range(3):
                        n = P if ch < 2 else TAIL
                        last = v_.tensor_tensor(
                            v_tok[0:n, ch, :].rearrange("p (a e) -> p a e", a=4),
                            ps[0:n, 4 + ch, :].rearrange("p (a e) -> p a e", a=4),
                            small[0:n, 3, 4 * ch:4 * ch + 4].unsqueeze(2).to_broadcast([n, 4, P]), ALU.mult)
                    last.then_inc(o_norm, 1)
                    out_of_psum("g0", g_out[:, 0:2, :], 0, used=9)
                    ahead(9)
                    out_of_psum("g1", g_out[:, 2:4, :], 2, used=10)
                    for kk in range(4):
                        low_y(kk + 1, kk, (y_tmp if kk < 2 else c_cu)[:, kk % 2, :])
                    v_.wait_ge(o_tr, m + 1)
                    v_.wait_ge(g_silu, m + 1)
                    for a in range(4):
                        v_.scalar_tensor_tensor(y_head[:, a, :], ps[:, 4 + a, 0:T], col("gla_norm", layer, a),
                                                g_out[:, a, :], ALU.mult, ALU.mult).then_inc(y_ready, 1)
                        if a > 0:
                            low_y(a + 4, 3 + a, y_head[:, a - 1, :])
                    low_y(8, 7, y_head[:, 3, :])
                    ahead(10)
                    ahead(11)
                    ahead(12)
                    sum_squares(1, t_end)
                    ahead(13)
                    sum_squares(2, t_end)
                v_.wait_ge(ss_post, bnd + 1)
                rsqrt(ps[:, 3, 0:T - t_end], D, ms[:, t_end:T], nt[:, t_end:T], r_post[:, t_end:T])
                final = bnd == NB - 1
                nx = phases[min(bnd + 1, NB - 1)]
                new_h(bnd + 1, POST[ph["kind"]], PRE[nx["kind"]], layer, nx["layer"], t_end, final)
            v_.wait_ge(ends_tr, 6)
            v_.tensor_copy(out_tok[:, 1, 512:1024], ps[:, 3, :]).then_inc(staged[3], 1)

        @block.gpsimd
        def _(pool):
            pool.memset(wp[:, :, :, :], 0.0).then_inc(zeroed, 1)
            pool.memset(small[:, :, :], 1.0)
            pool.sem_inc(hid_lo_ready, 1)
            pool.sem_inc(hid_lo_ready, 1)
            for ph in phases:
                bnd, t0 = ph["b"], ph["t_in"]
                for n, (a0, a1) in enumerate(((f[:, 0:2], f[:, 2:4]), (pre_acc, f[:, 4:6]), (pre_acc, f[:, 6:8]))):
                    pool.wait_ge(sq_ready, 8 * bnd + 2 * n + 4)
                    if n:
                        pool.wait_ge(pre_sum, 4 * bnd + n)
                    pool.tensor_tensor(pre_acc[:, :, t0:T], a0[:, :, t0:T], a1[:, :, t0:T], ALU.add).then_inc(pre_sum, 1)
                pool.wait_ge(pre_sum, 4 * bnd + 3)
                pool.tensor_tensor(pre_acc[:, 0, t0:T], pre_acc[:, 0, t0:T], pre_acc[:, 1, t0:T], ALU.add)\
                    .then_inc(pre_sum, 1)
                if ph["kind"] != "mix":
                    fi = ph["f"]

                    def group(parity, idx, dst_hi, dst_lo):
                        pool.wait_ge(silu_done, idx)
                        pool.wait_ge(up_evac, idx + 2)
                        pool.tensor_tensor(up[:, parity, :, t0:T], gate[:, parity, :, t0:T],
                                           up[:, parity, :, t0:T], ALU.mult).then_inc(hid_mul, 1)
                        pool.wait_ge(hid_hi_ready, idx)
                        pool.tensor_tensor(dst_lo, up[:, parity, :, t0:T], f32(dst_hi), ALU.subtract)\
                            .then_inc(hid_lo_ready, 1)

                    group(0, GROUPS * fi + 1, hid_hi[:, 0:2, t0:T], hid_lo[:, 0:2, t0:T])
                    with pool.Fori(0, GROUPS // 2) as i:
                        for g in (1, 2):
                            tiles = bass.ds(i * 4 + 2 * g, 2)
                            group(g % 2, i * 2 + (GROUPS * fi + g + 1), hid_hi[:, tiles, t0:T], hid_lo[:, tiles, t0:T])
                else:
                    m = ph["m"]
                    pool.wait_ge(pre_sum, 4 * bnd + 4)
                    pool.memset(s_diag[:, :, :, :, :], 0.0)
                    pool.memset(s_last[:, :, :, :], 0.0)
                    pool.memset(z_pad[:, :, 0:2], 0.0)
                    pool.memset(qd[:, 1], 0.0)
                    pool.memset(kd[:, 1], 0.0)
                    for w in (pool_in, win_a, win_b):
                        last = pool.memset(w[:, :, 0:PAD], 0.0)
                    last.then_inc(m_cleared, 1)
                    pool.wait_ge(m_cleared, m + 1)

                    def with_decays(j):
                        pool.wait_ge(dec_exp, JOBS * m + j + 1)
                        if j >= 2:
                            pool.wait_ge(job_mm, JOBS * m + j - 1)
                        d, qj, kj = dec[:, j % 2], qd[:, j % 2], kd[:, j % 2]
                        if j == 0:
                            pool.tensor_tensor(qj, q[:, :, :], d, ALU.mult)
                            pool.tensor_tensor(kj, k[:, :, :], inv_dec[:, :, :], ALU.mult).then_inc(qk_dec, 1)
                            return
                        if j < JOBS - 1:
                            bs = 2 * BASE << (j - 1)
                            n, hf = (T if T % bs == 0 else 2 * P), bs // 2
                            by = lambda x_: x_[:, :, 0:n].rearrange("p a (n s) -> p a n s", s=bs)
                            lt_, rt = (lambda x_: by(x_)[:, :, :, 0:hf]), (lambda x_: by(x_)[:, :, :, hf:bs])
                        else:
                            lt_, rt = (lambda x_: x_[:, :, 0:2 * P]), (lambda x_: x_[:, :, 2 * P:T])
                        pool.tensor_tensor(rt(qj), rt(q), rt(d), ALU.mult)
                        pool.tensor_tensor(lt_(kj), lt_(k), lt_(d), ALU.mult).then_inc(qk_dec, 1)

                    with_decays(0)
                    with_decays(1)
                    with_decays(2)
                    pool.wait_ge(m_evac, EVACS * m + OUT["pool"])
                    step = [8 * m]

                    def own(ins):
                        ins.then_inc(pool_own, 1)
                        step[0] += 1
                        pool.wait_ge(pool_own, step[0])
                    now = slice(PAD, PAD + T)
                    back = lambda n: slice(PAD - n, PAD - n + T)
                    lo_, hi_ = slice(0, 64), slice(64, P)
                    own(pool.tensor_tensor(win_a[:, :, now], pool_in[:, :, now], pool_in[:, :, back(1)], ALU.add))
                    own(pool.tensor_tensor(win_b[:, :, now], win_a[:, :, now], win_a[:, :, back(2)], ALU.add))
                    own(pool.tensor_tensor(y_tmp[lo_, 0, :], win_a[lo_, 0, now], inv_count[lo_, 0], ALU.mult))
                    own(pool.tensor_tensor(y_tmp[hi_, 0, :], win_b[hi_, 0, now], inv_count[hi_, 0], ALU.mult))
                    own(pool.tensor_tensor(win_a[:, 1, now], win_b[:, 1, now], win_b[:, 1, back(4)], ALU.add))
                    own(pool.tensor_tensor(y_tmp[lo_, 1, :], win_a[lo_, 1, now], inv_count[lo_, 1], ALU.mult))
                    own(pool.tensor_tensor(win_b[hi_, 1, now], win_a[hi_, 1, now], win_a[hi_, 1, back(8)], ALU.add))
                    own(pool.tensor_tensor(y_tmp[hi_, 1, :], win_b[hi_, 1, now], inv_count[hi_, 1], ALU.mult))
                    pool.tensor_tensor(y_tmp[:, :, :], y_tmp[:, :, :], pool_in[:, :, now], ALU.subtract)\
                        .then_inc(pool_win, 1)
                    assert step[0] == 8 * (m + 1)
                    for j in range(3, JOBS):
                        with_decays(j)

        @block.tensor
        def _(pe):
            def mm3(out_, wh, wl, xh, xl, first, last):
                pe.matmul(out_, wh, xh, start=first, stop=False)
                pe.matmul(out_, wh, xl, start=False, stop=False)
                return pe.matmul(out_, wl, xh, start=False, stop=last)

            def unit(slot, count, view, k_list, m_list, bank, xs, t0, k_first, k_last, high=None, low=None,
                     m_sets=None, after=None, before_last=None):
                pe.wait_ge(unit_lo, count)
                xh, xl = xs
                m_sets = m_sets or [m_list]
                for n, ms_ in enumerate(m_sets):
                    for kk, kg in enumerate(k_list):
                        if before_last and n == len(m_sets) - 1 and kk == len(k_list) - 1:
                            before_last()
                        outs = [ps[:, bank + mm, 0:T - t0] for mm in ms_]
                        if high:
                            pe.wait_ge(*high(kg))
                        for o, mm in zip(outs, ms_):
                            if not high:
                                last = mm3(o, view(w_hi, kk, mm), view(w_lo, kk, mm), xh[:, kg, t0:T], xl[:, kg, t0:T],
                                           kg == k_first, kg == k_last)
                            else:
                                pe.matmul(o, view(w_hi, kk, mm), xh[:, kg, t0:T], start=kg == k_first, stop=False)
                                pe.matmul(o, view(w_lo, kk, mm), xh[:, kg, t0:T], start=False, stop=False)
                        if high:
                            pe.wait_ge(*low(kg))
                            for o, mm in zip(outs, ms_):
                                last = pe.matmul(o, view(w_hi, kk, mm), xl[:, kg, t0:T], start=False, stop=kg == k_last)
                    if after and n < len(m_sets) - 1 and after[n] is not None:
                        last.then_inc(after[n], 1)
                last.then_inc(unit_used, 1)

            def up_view(slot):
                def view(w, kk, mm):
                    return w[:, slot].rearrange("p (s k n) -> p s k n", s=2, k=4)[:, mm // 2, kk, (mm % 2) * P:(mm % 2 + 1) * P]
                return view

            def k_view(slot, nk, n):
                def view(w, kk, mm):
                    return w[:, slot, 0:nk * n].rearrange("p (k n) -> p k n", k=nk)[:, kk, mm * P:(mm + 1) * P]
                return view

            def sum_h(ph, t0):
                pe.wait_ge(pre_sum, 4 * ph["b"] + 4)
                pe.matmul(ps[:, sum_bank(ph), 0:T - t0], ones[:, 0:P], pre_acc[:, 0, t0:T], start=True, stop=True)\
                  .then_inc(ss_pre, 1)

            def sum_f(blk, t0, part):
                if part == 0:
                    pe.wait_ge(sq_sum, 3 * blk + 3)
                else:
                    pe.wait_ge(sq_pair, 5 * blk + 3 + part)
                src = sq_new[:, part - 1, t0:T] if part else sq_acc[:, 0, t0:T]
                ins = pe.matmul(ps[:, 3, 0:T - t0], ones[:, 0:P], src, start=part == 0, stop=part == 2)
                if part == 2:
                    ins.then_inc(ss_post, 1)

            for _ in range(RING):
                pe.sem_inc(unit_used, 1)
            pe.wait_ge(par_in, 16 * (len(rows) + 1))
            pe.transpose(ps[:, 7, T:T + n_rows], par_rows[0:n_rows, :], ident[0:n_rows, 0:n_rows]).then_inc(ends_tr, 1)
            pe.wait_ge(x_in, 48)
            for kk in range(KT):
                if kk == KT - 1:
                    pe.wait_ge(par_ready, 1)
                pe.transpose(ps[:, kk, 0:NMETA], meta_tok[:, kk * P:(kk + 1) * P], ident[0:NMETA, 0:NMETA])
                for tt in range(2):
                    last = pe.transpose(ps[:, kk, NMETA + tt * P:NMETA + (tt + 1) * P],
                                        x_tok[:, tt, kk * P:(kk + 1) * P], ident)
            last.then_inc(ends_tr, 1)

            pe.wait_ge(ones_set, 1)
            for ph in phases:
                u0, layer, bnd, t0 = ph["u0"], ph["layer"], ph["b"], ph["t_in"]
                xs = (x_hi, x_lo)
                x_waits = dict(high=lambda kg: (xh_ready, 8 * bnd + kg + 1), low=lambda kg: (xl_ready, 8 * bnd + kg + 1))
                if ph["kind"] != "mix":
                    fi = ph["f"]

                    def group(parity, ja, i4, idx, **waits):
                        pe.wait_ge(up_evac, idx)
                        for j in range(2):
                            u = u0 + ja + j
                            unit(u % RING, i4 + (u + 1 + RING), up_view(u % RING), range(4 * j, 4 * j + 4), range(4),
                                 4 * parity, xs, t0, 0, KT - 1, **waits)

                    group(0, 0, 0, GROUPS * fi + 1, **x_waits)
                    sum_h(ph, t0)
                    pe.wait_ge(ms_read, bnd + 1)
                    with pe.Fori(0, GROUPS // 2) as i:
                        for g in (1, 2):
                            group(g % 2, 2 * g, i * 4, i * 2 + (GROUPS * fi + g + 1))
                    d0 = u0 + UP_UNITS
                    hid = (hid_hi, hid_lo)
                    pe.wait_ge(up_evac, GROUPS * fi + GROUPS + 1)

                    def hid_tile(kg):
                        return (hid_lo_ready, GROUPS * fi + kg // 2 + 1 + 2)
                    for pair in range(KT // 2):
                        if pair >= 2:
                            pe.wait_ge(pair_out, 4 * bnd + pair - 1)
                        k0 = 0
                        for j, nk in enumerate(DOWN_K):
                            u = d0 + 4 * pair + j
                            kw = {}
                            if pair == 0:
                                kw = dict(high=hid_tile, low=hid_tile)
                            if pair == 3 and j == 3:
                                sum_f(bnd, t0, 0)
                                kw = dict(m_sets=[[0], [1]], after=[tile_done], before_last=lambda: sum_f(bnd, t0, 1))
                            unit(u % RING, u + 1 + RING, k_view(u % RING, nk, 256), range(k0, k0 + nk), range(2),
                                 4 + 2 * (pair % 2), hid, t0, 0, FT - 1, **kw)
                            k0 += nk
                    sum_f(bnd, t0, 2)
                else:
                    m, t1 = ph["m"], ph["t_out"]

                    def proj(name, bank):
                        j = 2 + [n_ for n_, _, _ in PROJ].index(name)
                        n = PROJ[j - 2][2]
                        u = u0 + j
                        unit(u % RING, u + 1 + RING, k_view(u % RING, 8, n), range(8), range(n // P), bank, xs,
                             0, 0, KT - 1)

                    def wait_out(name):
                        pe.wait_ge(m_evac, EVACS * m + OUT[name])

                    for jj in range(2):
                        u = u0 + jj
                        unit(u % RING, u + 1 + RING, k_view(u % RING, 4, 512), range(4 * jj, 4 * jj + 4), range(4),
                             0, xs, 0, 0, KT - 1, **x_waits)
                    proj("glow", 4)
                    sum_h(ph, 0)
                    proj("v0", 6)
                    wait_out("qk")
                    pe.wait_ge(mix_in, 48)
                    for a in range(2):
                        last = pe.matmul(ps[:, a, 0:T], w2[:, layer, a * P:(a + 1) * P], glow, start=True, stop=True)
                    last.then_inc(z_mm, 1)
                    pe.wait_ge(ms_read, bnd + 1)
                    proj("v1", 4)
                    proj("pool", 2)
                    wait_out("v1")
                    for hh in range(HEADS):
                        for ch in range(2):
                            pe.transpose(ps[:, 4 + ch, hh * P:(hh + 1) * P], v[:, hh, ch * P:(ch + 1) * P], ident)
                        last = pe.matmul(ps[0:TAIL, 6, hh * P:(hh + 1) * P], v[:, hh, 2 * P:T], ident,
                                         start=True, stop=True)
                    last.then_inc(vt_mm, 1)
                    pe.wait_ge(z_out, m + 1)
                    proj("cb", 0)

                    def job(j):
                        bank = JOB_BANK[j]
                        pe.wait_ge(qk_dec, JOBS * m + j + 1)
                        for a in range(2):
                            for pr in range(2):
                                rows_ = slice(pr * 64, pr * 64 + 64)
                                kk, qq = kd[rows_, j % 2, a], qd[rows_, j % 2, a]

                                def score(out_, s, t):
                                    return pe.matmul(out_, kk[:, s], qq[:, t], start=True, stop=True)
                                for ch in range(2):
                                    o = ch * P
                                    if j < 6:
                                        last = score(ps[:, bank + 2 * ch + pr, a * P:(a + 1) * P],
                                                     slice(o, o + P), slice(o, o + P))
                                    elif j == 6:
                                        last = score(ps[0:64, bank + 2 * ch + pr, a * 64:(a + 1) * 64],
                                                     slice(o, o + 64), slice(o + 64, o + P))
                                    elif j == 7 and ch == 0:
                                        last = score(ps[:, bank + pr, a * P:(a + 1) * P], slice(0, P), slice(P, 2 * P))
                                    elif j == 8:
                                        at = (2 * ch + a) * TAIL
                                        last = score(ps[:, bank + pr, at:at + TAIL], slice(o, o + P), slice(2 * P, T))
                                if j < 4:
                                    at = 2 * P + a * TAIL
                                    last = score(ps[0:TAIL, bank + pr, at:at + TAIL], slice(2 * P, T), slice(2 * P, T))
                        last.then_inc(job_mm, 1)

                    def taken(n):
                        pe.wait_ge(cp_out, 6 * m + n)

                    pe.wait_ge(act_out, 4 * m + 1)
                    job(0)
                    wait_out("pool")
                    proj("cc", 2)
                    taken(1)
                    job(1)
                    wait_out("cb")
                    proj("cu", 0)
                    taken(2)
                    job(2)
                    wait_out("cc")
                    pe.wait_ge(pool_win, m + 1)
                    for a in range(2):
                        last = pe.matmul(ps[:, 2 + a, 0:T], wp[:, layer, a, :], y_tmp[:, a, :], start=True, stop=True)
                    last.then_inc(pool_mm, 1)
                    taken(3)
                    job(3)
                    wait_out("cu")
                    pe.wait_ge(y_ready, 8 * m + 4)
                    job(4)
                    for j in (5, 6, 7):
                        taken(j - 1)
                        job(j)
                    pe.wait_ge(act_out, 4 * m + 2)
                    job(8)
                    pe.wait_ge(act_out, 4 * m + 4)
                    for ch in range(3):
                        for hh in range(HEADS):
                            a, pr = hh // 2, hh % 2
                            n = P if ch < 2 else TAIL
                            parts = [(s_diag[:, 0, pr, a], 0)] if ch == 0 else \
                                [(s_next[:, hh, 0:P], 0), (s_diag[:, 1, pr, a], 1)] if ch == 1 else \
                                [(s_next[:, hh, P:P + TAIL], 0), (s_tail[:, hh], 1), (s_last[:, pr, a], 2)]
                            for n_, (sc, cs) in enumerate(parts):
                                vv = v_tok[:, cs] if cs < 2 else v_tok[0:TAIL, cs]
                                last = pe.matmul(ps[0:n, 4 + ch, hh * P:(hh + 1) * P], sc, vv[:, hh * P:(hh + 1) * P],
                                                 start=n_ == 0, stop=n_ == len(parts) - 1)
                    last.then_inc(o_mm, 1)

                    def out_unit(j, bank, **kw):
                        u = u0 + j
                        kh = 4 * ((j - 11) % 2)
                        unit(u % RING, u + 1 + RING, k_view(u % RING, 4, 512), range(kh, kh + 4), range(4),
                             bank, xs, t1, 0, KT - 1, **kw)
                    proj("g0", 0)
                    proj("g1", 2)
                    pe.wait_ge(o_norm, m + 1)
                    for hh in range(HEADS):
                        for ch in range(2):
                            pe.transpose(ps[:, 4 + hh, ch * P:(ch + 1) * P], v_tok[:, ch, hh * P:(hh + 1) * P], ident)
                        last = pe.transpose(ps[:, 4 + hh, 2 * P:T], v_tok[0:TAIL, 2, hh * P:(hh + 1) * P],
                                            ident[0:TAIL, 0:TAIL])
                    last.then_inc(o_tr, 1)
                    wait_out("g1")
                    y_waits = dict(high=lambda kg: (y_hi, 8 * m + kg + 1), low=lambda kg: (y_lo, 8 * m + kg + 1))
                    out_unit(11, 0, **y_waits)
                    out_unit(12, 0, **y_waits)
                    out_unit(13, 4)
                    out_unit(14, 4, m_sets=[[0, 1], [2], [3]], after=[half_done, tile_done],
                             before_last=lambda: (sum_f(bnd, t1, 0), sum_f(bnd, t1, 1)))
                    sum_f(bnd, t1, 2)
            for half in range(2):
                for tt in range(2):
                    for kk in range(4 * half, 4 * half + 4):
                        pe.wait_ge(h_ready, 8 * NB + kk + 1)
                        last = pe.transpose(ps[:, 2 * tt + half, (kk % 4) * P:(kk % 4 + 1) * P],
                                            h[:, kk, NMETA + tt * P:NMETA + (tt + 1) * P], ident)
                    last.then_inc(ends_tr, 1)


_INS = ["x", "meta", "ffn1_pre", "ffn1_post", "ffn1_wg", "ffn1_wu", "ffn1_wd", "mix_pre", "mix_post", "w_in",
        "pool_w", "pool_scale", "conv_w", "gla_w2", "gla_b2", "gla_norm", "w_out",
        "ffn2_pre", "ffn2_post", "ffn2_wg", "ffn2_wu", "ffn2_wd"]


def kernel(**inputs):
    import concourse.bacc as bacc
    from concourse.bass_utils import run_bass_kernel_spmd

    nc = bacc.Bacc("TRN2", target_bir_lowering=False, num_devices=1)
    arrays = {f"in_{n}": np.ascontiguousarray(inputs[n]) for n in _INS}
    arrays["in_consts"] = shape_constants(inputs["x"].shape[1] + NMETA)
    args = [nc.dram_tensor(n, a.shape, mybir.dt.from_np(a.dtype), kind="ExternalInput").ap()
            for n, a in arrays.items()]
    out = nc.dram_tensor("out", inputs["x"].shape, F32, kind="ExternalOutput").ap()
    trunk(nc, *args, out)
    r = run_bass_kernel_spmd(nc, [arrays], core_ids=[0])
    return r.results[0]["out"]
```

```python
from contextlib import ExitStack

import numpy as np
import concourse.bass as bass
from concourse import mybir

ALU = mybir.AluOpType
ACT = mybir.ActivationFunctionType
F32 = mybir.dt.float32
F32R = mybir.dt.float32r
I32 = mybir.dt.int32
U32 = mybir.dt.uint32

P = 128
NMETA = 16
D = 1024
KT = D // P
FF = 2816
FT = FF // P
GROUPS = FT // 2
HEADS = 4
EPS = 1e-6
RING = 4
UNIT = 2048
DOWN_K = (6, 6, 5, 5)
MAGIC = 1595932649.0
NEWTON = ((1.6819105, 0.70394764), (1.5000005, 0.50000016))
LOG_DECAY_MIN = -50.0
MIX_UNITS = 15
LATE = 4
WARM_START, WARM_BOUNDARY = 11, 6
C_QK = 1024
PROJ = (("glow", 2048, 128), ("v0", 1536, 256), ("pool", 0, 256), ("v1", 1792, 256), ("cb", 256, 256),
        ("cc", 512, 256), ("cu", 768, 256), ("g0", 2064, 256), ("g1", 2320, 256))
OUT = {name: n + 1 for n, name in enumerate(("glow", "qk", "v0", "pool", "v1", "cb", "cc", "cu", "g0", "g1"))}
EVACS = len(OUT)
JOB_BANK = (4, 4, 0, 0, 0, 4, 0, 4)
POOL_WINDOWS = (2, 4, 8, 16)
BASE = 4
LEVELS = (8, 16)
MASKED = 1 + len(LEVELS)
JOBS = MASKED + 5


def shape_constants(T):
    c = np.zeros((P, P + 2 * T + (1 + len(LEVELS)) * P), np.float32)
    c[:, 0:P] = np.eye(P)
    t = np.arange(T)
    for g, w in enumerate(POOL_WINDOWS):
        at = P + (g // 2) * T
        c[(g % 2) * 64:(g % 2) * 64 + 64, at:at + T] = 1.0 / np.minimum(t + 1, w)
    s, t = np.arange(P)[:, None], np.arange(P)[None, :]
    at = P + 2 * T
    c[:, at:at + P] = (s // BASE == t // BASE) & (s <= t)
    for n, bs in enumerate(LEVELS):
        at += P
        c[:, at:at + P] = (s // bs == t // bs) & (s % bs < bs // 2) & (t % bs >= bs // 2)
    return c


def trunk(nc, x, meta, ffn1_pre, ffn1_post, ffn1_wg, ffn1_wu, ffn1_wd, mix_pre, mix_post, w_in,
          pool_w, pool_scale, conv_w, gla_w2, gla_b2, gla_norm, w_out,
          ffn2_pre, ffn2_post, ffn2_wg, ffn2_wu, ffn2_wd, consts, out):
    SEQ = x.shape[1]
    T = SEQ + NMETA
    DEPTH = w_in.shape[0]
    TAIL = T - 2 * P

    FFN_UNITS = 2 * GROUPS + 4 * len(DOWN_K)
    phases = []
    u0 = 0
    for layer in range(DEPTH):
        for kind in ("ffn1", "mix", "ffn2"):
            last = layer == DEPTH - 1
            phases.append(dict(
                kind=kind, layer=layer, u0=u0, b=len(phases),
                f=2 * layer + (kind == "ffn2"),
                m=layer,
                t_in=NMETA if last and kind == "ffn2" else 0,
                t_out=NMETA if last and kind != "ffn1" else 0))
            u0 += MIX_UNITS if kind == "mix" else FFN_UNITS
    NB = len(phases)

    def weights(ph):
        wg, wu, wd = (ffn1_wg, ffn1_wu, ffn1_wd) if ph["kind"] == "ffn1" else (ffn2_wg, ffn2_wu, ffn2_wd)
        tiled = lambda w: w[ph["layer"]].rearrange("(k p) n -> p k n", p=P)
        return tiled(wg), tiled(wu), tiled(wd)

    ctx = ExitStack()
    with ctx:
        def sb(name, shape, dt=F32):
            return ctx.enter_context(nc.sbuf_tensor(name, shape, dt))

        def sem(name):
            return ctx.enter_context(nc.semaphore(name))

        h = sb("h", [P, KT, T])
        x_hi = sb("x_hi", [P, KT, T], F32R)
        x_lo = sb("x_lo", [P, KT, T], F32R)
        f = sb("f", [P, KT, T])
        raw = sb("raw", [P, RING, UNIT])
        w_hi = sb("w_hi", [P, RING, UNIT], F32R)
        w_lo = sb("w_lo", [P, RING, UNIT], F32R)
        cst = sb("cst", [P, P + 2 * T + (1 + len(LEVELS)) * P])
        ones = sb("ones", [P, T])
        par = sb("par", [P, P])
        r_post = sb("r_post", [P, T])
        r_pre = sb("r_pre", [P, T])
        ms = sb("ms", [P, T])
        eps = sb("eps", [P, 1])
        tables = sb("tables", [P, 32])
        w2 = sb("w2", [NMETA, DEPTH, 256])
        wp = sb("wp", [P, DEPTH, 2, P])
        ident = cst[:, 0:P]
        inv_count = cst[:, P:P + 2 * T].rearrange("p (a t) -> p a t", a=2)
        sq_acc = sb("sq_acc", [P, 2, T])
        sq_new = sb("sq_new", [P, 2, T])
        pre_acc = sb("pre_acc", [P, 2, T])
        small = sb("small", [P, 4, 12])

        def mask(n, rows):
            at = P + 2 * T + n * P
            return cst[0:rows, at:at + rows].bitcast(U32)

        ffn_floats = 2 * FT * T + 8 * T
        PAD = 16
        mix_floats = (6 * 2 + 4 + 4 * 4 + 4 + 4) * T + 1536 + 1024 + 4 * (P + TAIL) + 4 * TAIL \
            + 4 * TAIL + 2 * (2 + T) + 2 * T // BASE
        arena_bytes = 4 * max(ffn_floats, mix_floats)
        arena = sb("arena", [P, arena_bytes // 4])
        arena_at = nc.sbuf_base - arena_bytes
        laid = [0]

        def place(name, shape, dt=F32):
            n = 4 * int(np.prod(shape[1:]))
            t = nc.alloc_sbuf_tensor_at(name, shape, dt, offset=arena_at + laid[0])
            laid[0] += n
            assert laid[0] <= arena_bytes, (name, laid[0], arena_bytes)
            return t

        hid_hi = place("hid_hi", [P, FT, T], F32R)
        hid_lo = place("hid_lo", [P, FT, T], F32R)
        gate = place("gate", [P, 2, 2, T])
        up = place("up", [P, 2, 2, T])
        laid[0] = 0
        x_tok = place("x_tok", [P, 2, D])
        meta_tok = place("meta_tok", [NMETA, D])
        par_rows = place("par_rows", [P, P])
        out_tok = place("out_tok", [P, 2, D])
        laid[0] = 0
        q = place("q", [P, 2, 2, T])
        k = place("k", [P, 2, T])
        v = place("v", [P, 4, T])
        b = place("b", [P, 2, T])
        la = place("la", [P, 2, T])
        lt = place("lt", [P, 2, T])
        dec = place("dec", [P, 2, 2, T])
        qd = place("qd", [P, 2, 2, 2, T])
        kd = place("kd", [P, 2, 2, T])
        v_tok = place("v_tok", [P, 3, 512])
        s_diag = place("s_diag", [P, 2, HEADS, P])
        s_next = place("s_next", [P, 4, P + TAIL])
        s_tail = place("s_tail", [P, 4, TAIL])
        s_last = place("s_last", [TAIL, 4, TAIL])
        g_out = place("g_out", [P, 4, T])
        c_cu = place("c_cu", [P, 4, T])
        mid = place("mid", [P, 2, T // BASE])
        z_pad = place("z_pad", [P, 2, 2 + T])
        glow = z_pad[0:NMETA, 0, 2:2 + T]
        y_tmp = sq_new
        inv_dec = lt
        c_b = lt
        y_head = v
        f_flat = f[:, :, :].rearrange("p k t -> p (k t)")
        n_win = 2 * (PAD + T)
        pool_in, win_a, win_b = (f_flat[:, i * n_win:(i + 1) * n_win].rearrange("p (a t) -> p a t", a=2)
                                 for i in range(3))

        ps = ctx.enter_context(nc.psum_tensor("ps", [P, 8, 512], F32))

        raw_in = [sem(f"raw_in{i}") for i in range(RING)]
        unit_hi = sem("unit_hi")
        unit_lo = sem("unit_lo")
        unit_used = sem("unit_used")
        ident_in = sem("ident_in")
        gain_in = sem("gain_in")
        par_in = sem("par_in")
        masks_in = sem("masks_in")
        mix_in = sem("mix_in")
        x_in = sem("x_in")
        zeroed = sem("zeroed")
        ones_set = sem("ones_set")
        ends_tr = sem("ends_tr")
        staged = [sem(f"staged{i}") for i in range(4)]
        par_ready = sem("par_ready")
        h_ready = sem("h_ready")
        xh_ready = sem("xh_ready")
        xl_ready = sem("xl_ready")
        sq_ready = sem("sq_ready")
        pre_sum = sem("pre_sum")
        ss_pre = sem("ss_pre")
        pre_root = sem("pre_root")
        post_root = sem("post_root")
        eps_set = sem("eps_set")
        r_out = sem("r_out")
        late_scaled = sem("late_scaled")
        dve = sem("dve")
        gate_ready = sem("gate_ready")
        silu_done = sem("silu_done")
        up_evac = sem("up_evac")
        hid_mul = sem("hid_mul")
        hid_hi_ready = sem("hid_hi_ready")
        hid_lo_ready = sem("hid_lo_ready")
        pair_out = sem("pair_out")
        sq_pair = sem("sq_pair")
        sq_sum = sem("sq_sum")
        ss_post = sem("ss_post")
        done_out = sem("done_out")
        m_evac = sem("m_evac")
        m_cleared = sem("m_cleared")
        half_done = sem("half_done")
        tile_done = sem("tile_done")
        z_mm = sem("z_mm")
        z_out = sem("z_out")
        lt_step = sem("lt_step")
        dec_arg = sem("dec_arg")
        dec_exp = sem("dec_exp")
        q_dec = sem("q_dec")
        k_dec = sem("k_dec")
        job_mm = sem("job_mm")
        vt_mm = sem("vt_mm")
        act_out = sem("act_out")
        inv_exp = sem("inv_exp")
        cp_out = sem("cp_out")
        g_silu = sem("g_silu")
        pool_win = sem("pool_win")
        pool_own = sem("pool_own")
        pool_mm = sem("pool_mm")
        y_ready = sem("y_ready")
        y_hi = sem("y_hi")
        y_lo = sem("y_lo")
        o_mm = sem("o_mm")
        o_sq = sem("o_sq")
        o_norm = sem("o_norm")
        o_tr = sem("o_tr")

        block = ctx.enter_context(nc.Block())

        C = {}
        rows = [("ffn1_pre", ffn1_pre, KT), ("ffn1_post", ffn1_post, KT), ("mix_pre", mix_pre, KT),
                ("mix_post", mix_post, KT), ("ffn2_pre", ffn2_pre, KT), ("ffn2_post", ffn2_post, KT),
                ("pool_scale", pool_scale, 2), ("conv_w", conv_w, 6), ("gla_b2", gla_b2, 2),
                ("gla_norm", gla_norm, 4)]
        n_rows = 0
        for name, _, per in rows:
            C[name] = (n_rows, per)
            n_rows += DEPTH * per

        n_first = DEPTH * rows[0][2]

        def col(name, layer, i):
            base, per = C[name]
            c = base + layer * per + i
            return par[:, c:c + 1]

        def load_rows(eng, name, src, per, landed):
            r0 = C[name][0]
            if name == "conv_w":
                by_tile = src.rearrange("l j (a p) -> (l j a) p", p=P)
            else:
                by_tile = src.rearrange("l (a p) -> (l a) p", p=P)
            eng.dma_start(par_rows[r0:r0 + DEPTH * per, :], by_tile).then_inc(landed, 16)

        def f32(ap):
            return ap.bitcast(F32)

        def sum_bank(ph):
            return 5 if ph["kind"] == "mix" else 4

        def last_of(ph, what):
            return ph["u0"] + what + 1 + RING

        UP_UNITS = 2 * GROUPS
        MIX_SIZE = [UNIT] * 2 + [1024] + [UNIT] * 12

        @block.sync
        def _(sp):
            def load(slot, value, *copies):
                sp.wait_ge(unit_lo, value)
                for dst, src in copies:
                    sp.dma_start(dst, src).then_inc(raw_in[slot], 16)

            def first_loads():
                sp.dma_start(meta_tok[:, :], meta).then_inc(x_in, 16)
                for tt in range(2):
                    sp.dma_start(x_tok[:, tt], x[0, tt * P:(tt + 1) * P, :]).then_inc(x_in, 16)
                for name, src, per in rows[1:]:
                    load_rows(sp, name, src, per, par_in)

            def constant_loads():
                sp.dma_start(cst[:, P:], consts[:, P:]).then_inc(masks_in, 16)
                sp.dma_start(w2[:, :, :], gla_w2.rearrange("l r n -> r l n")).then_inc(mix_in, 16)
                sp.wait_ge(zeroed, 1)
                for g in range(2):
                    sp.dma_start(wp[g * 64:g * 64 + 64, :, :, g * 64:g * 64 + 64].rearrange("c l a d -> c (l a) d"),
                                 pool_w.rearrange("l (a g) c d -> g c (l a) d", g=2)[g]).then_inc(mix_in, 16)

            for ph in phases:
                u0, layer = ph["u0"], ph["layer"]
                if ph["kind"] != "mix":
                    wg, wu, wd = weights(ph)

                    def up_unit(j, value, cols):
                        slot = (u0 + j) % RING
                        dst = raw[:, slot].rearrange("p (s k n) -> p s k n", s=2, k=4)
                        ks = slice(4 * (j % 2), 4 * (j % 2) + 4)
                        load(slot, value, (dst[:, 0], wg[:, ks, cols]), (dst[:, 1], wu[:, ks, cols]))

                    for j in range(2):
                        up_unit(j, u0 + j + 1, slice(0, 256))
                        if j == 0 and u0 == 0:
                            first_loads()
                        if j == 1 and u0 == 0:
                            constant_loads()
                    with sp.Fori(0, GROUPS // 2) as i:
                        for j in range(4):
                            up_unit(2 + j, i * 4 + (u0 + 2 + j + 1), bass.ds(i * 512 + 256 + 256 * (j // 2), 256))
                    with sp.Fori(0, KT // 2) as i:
                        k0 = 0
                        for j, nk in enumerate(DOWN_K):
                            slot = (u0 + UP_UNITS + j) % RING
                            dst = raw[:, slot, 0:nk * 256].rearrange("p (k n) -> p k n", k=nk)
                            cols = bass.ds(i * 256, 256)
                            load(slot, i * 4 + (u0 + UP_UNITS + j + 1),
                                 (dst[:, 0:3], wd[:, k0:k0 + 3, cols]), (dst[:, 3:nk], wd[:, k0 + 3:k0 + nk, cols]))
                            k0 += nk
                else:
                    wi = w_in[layer].rearrange("(k p) n -> p k n", p=P)
                    wo = w_out[layer].rearrange("(k p) n -> p k n", p=P)

                    def block_unit(j, w, k0, nk, c0, n):
                        slot = (u0 + j) % RING
                        dst = raw[:, slot, 0:nk * n].rearrange("p (k n) -> p k n", k=nk)
                        half = nk // 2
                        load(slot, u0 + j + 1, (dst[:, 0:half], w[:, k0:k0 + half, c0:c0 + n]),
                             (dst[:, half:nk], w[:, k0 + half:k0 + nk, c0:c0 + n]))
                    block_unit(0, wi, 0, 4, C_QK, 512)
                    block_unit(1, wi, 4, 4, C_QK, 512)
                    for j, (_, c0, n) in enumerate(PROJ):
                        block_unit(2 + j, wi, 0, 8, c0, n)
                    for j in range(4):
                        block_unit(11 + j, wo, 4 * (j % 2), 4, 512 * (j // 2), 512)
            for n, (half, tt) in enumerate(((0, 0), (0, 1), (1, 0), (1, 1))):
                cols = slice(half * 512, half * 512 + 512)
                sp.wait_ge(staged[n], 1)
                sp.dma_start(out[0, tt * P:(tt + 1) * P, cols], out_tok[:, tt, cols]).then_inc(done_out, 16)
            sp.wait_ge(done_out, 64)

        @block.scalar
        def _(act):
            dummies = iter(range(tables.shape[1]))

            def load_table(function):
                n = next(dummies)
                act.activation(tables[:, n:n + 1], ones[:, 0:1], function)

            act.dma_start(cst[:, 0:P], consts[:, 0:P]).then_inc(ident_in, 16)
            load_rows(act, *rows[0], gain_in)
            act.wait_ge(ones_set, 1)
            load_table(ACT.Copy)

            def high(slot, n, arrived, free):
                act.wait_ge(raw_in[slot], arrived)
                act.wait_ge(unit_used, free)
                act.activation(w_hi[:, slot, 0:n], raw[:, slot, 0:n], ACT.Copy).then_inc(unit_hi, 1)

            def high_unit(u, n):
                high(u % RING, n, 32 * (u // RING + 1), u + 1)

            def split_h(bnd, gain, layer, t0):
                for kk in range(KT):
                    act.wait_ge(h_ready, 8 * bnd + kk + 1)
                    act.activation(x_hi[:, kk, t0:T], h[:, kk, t0:T], ACT.Copy,
                                   scale=col(gain, layer, kk)).then_inc(xh_ready, 1)
                    act.activation(f[:, kk, t0:T], h[:, kk, t0:T], ACT.Square).then_inc(sq_ready, 1)

            def pair_evac(blk, pair, bank, t0, sem_, count):
                src = ps[:, bank:bank + 2, 0:T - t0]
                if pair < 3:
                    act.wait_ge(sem_, count)
                    if pair == 2:
                        act.wait_ge(sq_sum, 3 * blk + 1)
                    dst = sq_acc if pair == 0 else sq_new
                    act.activation(dst[:, :, t0:T], src, ACT.Square).then_inc(sq_pair, 1)
                else:
                    act.wait_ge(sq_sum, 3 * blk + 2)
                    act.wait_ge(tile_done, blk + 1)
                    act.activation(sq_new[:, 0, t0:T], src[:, 0], ACT.Square).then_inc(sq_pair, 1)
                    act.wait_ge(sem_, count)
                    act.activation(sq_new[:, 1, t0:T], src[:, 1], ACT.Square).then_inc(sq_pair, 1)
                act.activation(f[:, 2 * pair:2 * pair + 2, t0:T], src, ACT.Copy).then_inc(pair_out, 1)

            def high_x(kk):
                act.wait_ge(h_ready, kk + 1)
                act.activation(x_hi[:, kk, :], h[:, kk, :], ACT.Copy, scale=col("ffn1_pre", 0, kk)).then_inc(xh_ready, 1)

            high_unit(0, UNIT)
            act.wait_ge(par_ready, 1)
            for kk in range(KT):
                high_x(kk)
            high_unit(1, UNIT)
            for kk in range(KT):
                act.activation(f[:, kk, :], h[:, kk, :], ACT.Square).then_inc(sq_ready, 1)
            act.wait_ge(eps_set, 1)
            load_table(ACT.Sqrt)
            for ph in phases:
                u0, layer, bnd, t0 = ph["u0"], ph["layer"], ph["b"], ph["t_in"]
                if bnd:
                    split_h(bnd, {"ffn1": "ffn1_pre", "mix": "mix_pre", "ffn2": "ffn2_pre"}[ph["kind"]], layer, t0)
                for u in range(3 if bnd else 2, RING):
                    high_unit(u0 + u, UNIT)

                def pre_rms():
                    act.wait_ge(ss_pre, bnd + 1)
                    act.activation(ms[:, t0:T], ps[:, sum_bank(ph), 0:T - t0], ACT.Sqrt, bias=eps[:, :],
                                   scale=1.0 / D).then_inc(pre_root, 1)
                if ph["kind"] != "mix":
                    fi = ph["f"]

                    def group(parity, ua, i4, i32, idx, dst, first=False):
                        if first and bnd == 0:
                            pre_rms()
                        high(ua % RING, UNIT, i32 + 32 * (ua // RING + 1), i4 + (ua + 1))
                        if first and bnd:
                            pre_rms()
                        if first:
                            load_table(ACT.Silu)
                        act.wait_ge(gate_ready, idx)
                        act.activation(gate[:, parity, :, t0:T], gate[:, parity, :, t0:T], ACT.Silu)\
                           .then_inc(silu_done, 1)
                        high((ua + 1) % RING, UNIT, i32 + 32 * ((ua + 1) // RING + 1), i4 + (ua + 2))
                        act.wait_ge(hid_mul, idx)
                        act.activation(dst, up[:, parity, :, t0:T], ACT.Copy).then_inc(hid_hi_ready, 1)

                    group(0, u0 + RING, 0, 0, GROUPS * fi + 1, hid_hi[:, 0:2, t0:T], first=True)
                    with act.Fori(0, GROUPS // 2) as i:
                        for g in (1, 2):
                            group(g % 2, u0 + 2 * g + RING, i * 4, i * 32, i * 2 + (GROUPS * fi + g + 1),
                                  hid_hi[:, bass.ds(i * 4 + 2 * g, 2), t0:T])
                    d0 = u0 + UP_UNITS
                    for pair in range(KT // 2):
                        last_pair = pair == KT // 2 - 1
                        if last_pair:
                            load_table(ACT.Sqrt)
                        for j in range(4):
                            u = d0 + 4 * pair + j + RING
                            if not last_pair:
                                high_unit(u, DOWN_K[j] * 256)
                            elif j < 3 and bnd < NB - 1:
                                high_unit(u, UNIT)
                        pair_evac(bnd, pair, 4 + 2 * (pair % 2), t0, unit_used, last_of(ph, UP_UNITS + 4 * pair + 3))
                else:
                    m, t1 = ph["m"], ph["t_out"]

                    def ahead(j):
                        high_unit(u0 + j + RING, MIX_SIZE[j + RING] if j + RING < MIX_UNITS else UNIT)

                    def decays(j):
                        act.wait_ge(dec_arg, JOBS * m + j + 1)
                        n = T if j < MASKED or j == JOBS - 1 else 2 * P
                        if j == 0:
                            act.activation(inv_dec[:, :, :], dec[:, 0], ACT.Exp, scale=-1.0).then_inc(inv_exp, 1)
                            act.wait_ge(inv_exp, m + 1)
                        act.activation(dec[:, j % 2, :, 0:n], dec[:, j % 2, :, 0:n], ACT.Exp).then_inc(dec_exp, 1)

                    def scores_out(j):
                        act.wait_ge(job_mm, JOBS * m + j + 1)
                        bank = JOB_BANK[j]
                        if j < JOBS - 2:
                            bs = 2 * BASE << (j - 1)
                            hf = bs // 2
                            for o in range(0, P, bs):
                                src = ps[o:o + hf, bank:bank + 4, 0:bs].rearrange("p b (r t) -> p b r t", r=2)
                                dst = s_diag[o:o + hf, :, :, :].rearrange("p c (a r) t -> p (c a) r t", r=2)
                                last = act.activation(dst[:, :, :, o + hf:o + bs], src, ACT.Copy)
                        elif j == JOBS - 2:
                            last = act.activation(
                                s_next[:, :, 0:P].rearrange("p (a r) t -> p a r t", r=2),
                                ps[:, bank:bank + 2, 0:2 * P].rearrange("p a (r t) -> p a r t", r=2), ACT.Copy)
                        else:
                            src = ps[:, bank:bank + 2, 0:4 * TAIL].rearrange("p c (h t) -> p c h t", h=HEADS)
                            act.activation(s_next[:, :, P:P + TAIL], src[:, 0], ACT.Copy)
                            last = act.activation(s_tail[:, :, :], src[:, 1], ACT.Copy)
                        last.then_inc(act_out, 1)

                    ahead(0)
                    ahead(1)
                    pre_rms()
                    ahead(2)
                    ahead(3)
                    load_table(ACT.Exp)
                    act.wait_ge(z_out, m + 1)
                    act.activation(lt[:, :, :], la[:, :, :], ACT.Abs).then_inc(lt_step, 1)
                    act.wait_ge(lt_step, 3 * m + 1)
                    act.activation(lt[:, :, :], lt[:, :, :], ACT.Exp, scale=-1.0).then_inc(lt_step, 1)
                    act.wait_ge(lt_step, 3 * m + 2)
                    act.activation(lt[:, :, :], lt[:, :, :], ACT.Ln, bias=1.0).then_inc(lt_step, 1)
                    load_table(ACT.Exp)
                    ahead(4)
                    decays(0)
                    decays(1)
                    ahead(5)
                    act.wait_ge(vt_mm, m + 1)
                    act.activation(v_tok[:, 0:2, :], ps[:, 4:6, :], ACT.Copy)
                    act.activation(v_tok[0:TAIL, 2, :], ps[0:TAIL, 6, :], ACT.Copy).then_inc(act_out, 1)
                    decays(2)
                    ahead(6)
                    decays(3)
                    decays(4)
                    ahead(7)
                    decays(5)
                    decays(6)
                    act.wait_ge(m_cleared, m + 1)
                    scores_out(3)
                    scores_out(4)
                    decays(7)
                    scores_out(5)
                    scores_out(6)
                    scores_out(7)
                    ahead(8)
                    act.wait_ge(o_mm, m + 1)
                    sq_o = qd[:, 0].rearrange("p a b t -> p (a b t)")
                    act.activation(sq_o[:, 0:1024].rearrange("p (c n) -> p c n", c=2), ps[:, 4:6, :], ACT.Square)
                    act.activation(kd[:, :, :, :].rearrange("p a b t -> p (a b t)")[0:TAIL, 0:512], ps[0:TAIL, 6, :],
                                   ACT.Square).then_inc(o_sq, 1)
                    ahead(9)
                    load_table(ACT.Silu)
                    act.wait_ge(unit_used, last_of(ph, 10))

                    def high_y(n, kk, src):
                        act.wait_ge(y_ready, 8 * m + n)
                        act.activation(x_hi[:, kk, :], src, ACT.Copy).then_inc(y_hi, 1)
                    for kk in range(4):
                        high_y(4, kk, (y_tmp if kk < 2 else c_cu)[:, kk % 2, :])
                    act.wait_ge(m_evac, EVACS * m + OUT["g1"])
                    act.activation(g_out[:, :, :], g_out[:, :, :], ACT.Silu).then_inc(g_silu, 1)
                    for a in range(4):
                        high_y(a + 5, 4 + a, y_head[:, a, :])
                    ahead(10)
                    ahead(11)
                    ahead(12)
                    load_table(ACT.Sqrt)
                    for pair in range(2):
                        pair_evac(bnd, pair, 2 * pair, t1, unit_used, last_of(ph, 12))
                    ahead(13)
                    pair_evac(bnd, 2, 4, t1, half_done, m + 1)
                    pair_evac(bnd, 3, 6, t1, unit_used, last_of(ph, 14))
                t_end = ph["t_out"] if ph["kind"] == "mix" else t0
                act.wait_ge(ss_post, bnd + 1)
                act.activation(r_post[:, t_end:T], ps[:, 3, 0:T - t_end], ACT.Sqrt, bias=eps[:, :],
                               scale=1.0 / D).then_inc(post_root, 1)
            for n, bank in enumerate((0, 2, 1)):
                act.wait_ge(ends_tr, 2 + KT + n + 1)
                act.activation(out_tok[:, bank // 2, (bank % 2) * 512:(bank % 2 + 1) * 512], ps[:, bank, :], ACT.Copy)\
                   .then_inc(staged[n], 1)

        @block.vector
        def _(v_):
            own = [0]

            def mark(ins):
                ins.then_inc(dve, 1)
                own[0] += 1
                return own[0]

            def low(slot, n, count):
                v_.wait_ge(unit_hi, count)
                v_.tensor_tensor(w_lo[:, slot, 0:n], raw[:, slot, 0:n], f32(w_hi[:, slot, 0:n]), ALU.subtract)\
                  .then_inc(unit_lo, 1)

            def low_unit(u, n):
                low(u % RING, n, u + 1)

            def rsqrt(src, n, mean, tmp, dst):
                c = mark(v_.tensor_scalar(mean, src, 1.0 / n, EPS, ALU.mult, ALU.add))
                v_.wait_ge(dve, c)
                c = mark(v_.tensor_scalar(dst.bitcast(I32), mean.bitcast(I32), -0.5, MAGIC, ALU.mult, ALU.add))
                for plus, minus in NEWTON:
                    v_.wait_ge(dve, c)
                    c = mark(v_.tensor_tensor(tmp, dst, dst, ALU.mult))
                    v_.wait_ge(dve, c)
                    c = mark(v_.scalar_tensor_tensor(tmp, tmp, -minus, mean, ALU.mult, ALU.mult))
                    v_.wait_ge(dve, c)
                    c = mark(v_.scalar_tensor_tensor(dst, tmp, plus, dst, ALU.add, ALU.mult))
                v_.wait_ge(dve, c)

            def tok(r, a, t0):
                return r[:, t0:T].unsqueeze(1).to_broadcast([P, a, T - t0])

            def new_h(bnd, post, pre, layer, layer_pre, t0, final):
                def low_x(kk):
                    v_.wait_ge(xh_ready, 8 * bnd + kk + 1)
                    v_.scalar_tensor_tensor(x_lo[:, kk, t0:T], h[:, kk, t0:T], col(pre, layer_pre, kk),
                                            f32(x_hi[:, kk, t0:T]), ALU.mult, ALU.subtract).then_inc(xl_ready, 1)
                c = {}

                def scale(kk, n):
                    v_.wait_ge(pair_out, 4 * (bnd - 1) + kk // 2 + 1)
                    c[kk] = c[kk + n - 1] = mark(v_.tensor_tensor(
                        f[:, kk:kk + n, t0:T], f[:, kk:kk + n, t0:T], tok(r_post, n, t0), ALU.mult))

                def add(kk):
                    if final and kk >= LATE:
                        v_.wait_ge(late_scaled, (kk - LATE) // 2 + 1)
                    else:
                        v_.wait_ge(dve, c[kk])
                    v_.scalar_tensor_tensor(h[:, kk, t0:T], f[:, kk, t0:T], col(post, layer, kk),
                                            h[:, kk, t0:T], ALU.mult, ALU.add).then_inc(h_ready, 1)
                for kk in range(KT):
                    if kk < 2:
                        scale(kk, 1)
                    elif kk % 2 == 0 and not (final and kk >= LATE):
                        scale(kk, 2)
                    if kk > 1 and not final:
                        low_x(kk - 2)
                    add(kk)
                if not final:
                    low_x(KT - 2)
                    low_x(KT - 1)

            def other_parameters():
                v_.wait_ge(ends_tr, 1 + KT + 1)
                c = mark(v_.tensor_copy(par[:, n_first:n_rows], ps[:, 6, T + n_first:T + n_rows]))
                v_.wait_ge(dve, c)
                for name in ("ffn1_post", "ffn2_post"):
                    cs = slice(C[name][0], C[name][0] + DEPTH * KT)
                    last = v_.tensor_scalar(par[:, cs], par[:, cs], 0.5, None, ALU.mult)
                c = mark(last)
                v_.wait_ge(dve, c)
                v_.sem_inc(par_ready, 1)

            v_.memset(ones[:, :], 1.0).then_inc(ones_set, 1)
            v_.memset(eps[:, :], EPS).then_inc(eps_set, 1)
            for _ in range(RING):
                v_.sem_inc(unit_lo, 1)
            v_.sem_inc(up_evac, 1)
            v_.sem_inc(up_evac, 1)
            low_unit(0, UNIT)
            v_.wait_ge(ends_tr, 1)
            v_.tensor_copy(par[:, 0:n_first], ps[:, 7, T:T + n_first]).then_inc(par_ready, 1)

            def low_x(kk):
                v_.wait_ge(xh_ready, kk + 1)
                v_.scalar_tensor_tensor(x_lo[:, kk, :], h[:, kk, :], col("ffn1_pre", 0, kk),
                                        f32(x_hi[:, kk, :]), ALU.mult, ALU.subtract).then_inc(xl_ready, 1)
            for kk in range(KT):
                v_.wait_ge(ends_tr, kk + 2)
                v_.tensor_copy(h[:, kk, :], ps[:, kk, 0:T]).then_inc(h_ready, 1)
            for kk in range(KT - 1):
                low_x(kk)
            low_unit(1, UNIT)
            low_x(KT - 1)
            POST = {"ffn1": "ffn1_post", "mix": "mix_post", "ffn2": "ffn2_post"}
            PRE = {"ffn1": "ffn1_pre", "mix": "mix_pre", "ffn2": "ffn2_pre"}
            for ph in phases:
                u0, layer, bnd, t0 = ph["u0"], ph["layer"], ph["b"], ph["t_in"]
                low_unit(u0 + (3 if bnd else 2), UNIT)

                def pre_rms():
                    v_.wait_ge(pre_root, bnd + 1)
                    c = mark(v_.reciprocal(r_pre[:, t0:T], ms[:, t0:T]))
                    v_.wait_ge(dve, c)

                def sum_squares(pair, ts):
                    v_.wait_ge(sq_pair, 5 * bnd + pair + 1)
                    v_.tensor_tensor(sq_acc[:, :, ts:T], sq_acc[:, :, ts:T], sq_new[:, :, ts:T], ALU.add)\
                      .then_inc(sq_sum, 1)
                    if pair == 2:
                        v_.wait_ge(sq_sum, 3 * bnd + 2)
                        v_.tensor_tensor(sq_acc[:, 0, ts:T], sq_acc[:, 0, ts:T], sq_acc[:, 1, ts:T], ALU.add)\
                          .then_inc(sq_sum, 1)

                if ph["kind"] != "mix":
                    fi = ph["f"]

                    def group(parity, ua, i4, idx, first=False):
                        if first and bnd == 0:
                            other_parameters()
                            pre_rms()
                            low_unit(3, UNIT)
                        low(ua % RING, UNIT, i4 + (ua + 1))
                        if first and bnd:
                            pre_rms()
                        v_.wait_ge(unit_used, i4 + (ua + 2))
                        v_.wait_ge(hid_lo_ready, idx)
                        bank = 4 * parity
                        v_.tensor_tensor(gate[:, parity, :, t0:T], ps[:, bank:bank + 2, 0:T - t0],
                                         tok(r_pre, 2, t0), ALU.mult).then_inc(gate_ready, 1)
                        v_.tensor_tensor(up[:, parity, :, t0:T], ps[:, bank + 2:bank + 4, 0:T - t0],
                                         tok(r_pre, 2, t0), ALU.mult).then_inc(up_evac, 1)
                        low((ua + 1) % RING, UNIT, i4 + (ua + 2))

                    group(0, u0 + RING, 0, GROUPS * fi + 1, first=True)
                    with v_.Fori(0, GROUPS // 2) as i:
                        for g in (1, 2):
                            group(g % 2, u0 + 2 * g + RING, i * 4, i * 2 + (GROUPS * fi + g + 1))
                    d0 = u0 + UP_UNITS
                    for pair in range(KT // 2):
                        last_pair = pair == KT // 2 - 1
                        for j in range(4):
                            u = d0 + 4 * pair + j + RING
                            if not last_pair:
                                low_unit(u, DOWN_K[j] * 256)
                            elif j < 3 and bnd < NB - 1:
                                low_unit(u, UNIT)
                        if pair in (1, 2):
                            sum_squares(pair, t0)
                    t_end = t0
                else:
                    m, t_end = ph["m"], ph["t_out"]

                    def ahead(j):
                        low_unit(u0 + j + RING, MIX_SIZE[j + RING] if j + RING < MIX_UNITS else UNIT)

                    def by_block(x_, bs, n):
                        return x_[:, :, 0:n].rearrange("p a (n s) -> p a n s", s=bs)

                    def exponents(j):
                        if j >= 2:
                            v_.wait_ge(q_dec, JOBS * m + j - 1)
                            v_.wait_ge(k_dec, JOBS * m + j - 1)
                        d = dec[:, j % 2]
                        if j == 0:
                            bb = by_block(b, BASE, T)
                            c = mark(v_.tensor_tensor(mid[:, :, :], bb[:, :, :, 0], bb[:, :, :, BASE - 1], ALU.add))
                            v_.wait_ge(dve, c)
                            ref = mid[:, :, :].unsqueeze(3).to_broadcast([P, 2, T // BASE, BASE])
                            v_.scalar_tensor_tensor(by_block(d, BASE, T), ref, -0.5, bb, ALU.mult, ALU.add)\
                              .then_inc(dec_arg, 1)
                        elif j < JOBS - 1:
                            bs = 2 * BASE << (j - 1)
                            n = T if T % bs == 0 else 2 * P
                            bb, dd, hf = by_block(b, bs, n), by_block(d, bs, n), bs // 2
                            ref = bb[:, :, :, hf - 1:hf].to_broadcast([P, 2, n // bs, hf])
                            v_.tensor_tensor(dd[:, :, :, 0:hf], ref, bb[:, :, :, 0:hf], ALU.subtract)
                            v_.tensor_tensor(dd[:, :, :, hf:bs], bb[:, :, :, hf:bs], ref, ALU.subtract)\
                              .then_inc(dec_arg, 1)
                        else:
                            ref = b[:, :, 2 * P - 1:2 * P]
                            v_.tensor_tensor(d[:, :, 0:2 * P], ref.to_broadcast([P, 2, 2 * P]), b[:, :, 0:2 * P],
                                             ALU.subtract)
                            v_.tensor_tensor(d[:, :, 2 * P:T], b[:, :, 2 * P:T], ref.to_broadcast([P, 2, TAIL]),
                                             ALU.subtract).then_inc(dec_arg, 1)

                    def keys_of(j):
                        if j == 0:
                            return lambda x_: x_[:, :, :]
                        if j == JOBS - 1:
                            return (lambda x_: x_[:, :, 0:2 * P])
                        bs = 2 * BASE << (j - 1)
                        n, hf = (T if T % bs == 0 else 2 * P), bs // 2
                        return (lambda x_: by_block(x_, bs, n)[:, :, :, 0:hf])

                    def k_decay(j):
                        v_.wait_ge(dec_exp, JOBS * m + j + 1)
                        if j >= 2:
                            v_.wait_ge(job_mm, JOBS * m + j - 1)
                        keys = keys_of(j)
                        d = dec[:, j % 2] if j else inv_dec
                        v_.tensor_tensor(keys(kd[:, j % 2]), keys(k), keys(d), ALU.mult).then_inc(k_dec, 1)

                    def take_scores(j):
                        v_.wait_ge(job_mm, JOBS * m + j + 1)
                        bank = JOB_BANK[j]
                        src = ps[:, bank:bank + 4, 0:2 * P].rearrange("p b (r t) -> p b r t", r=2)
                        dst = s_diag[:, :, :, :].rearrange("p c (a r) t -> p (c a) r t", r=2)
                        if j:
                            v_.wait_ge(cp_out, MASKED * m + j)
                        v_.copy_predicated(dst, mask(j, P).unsqueeze(1).unsqueeze(1).to_broadcast([P, 4, 2, P]), src)
                        last = v_.copy_predicated(
                            s_last[:, :, :].rearrange("p (a r) t -> p a r t", r=2),
                            mask(j, TAIL).unsqueeze(1).unsqueeze(1).to_broadcast([TAIL, 2, 2, TAIL]),
                            ps[0:TAIL, bank:bank + 2, 2 * P:2 * P + 2 * TAIL].rearrange("p b (r t) -> p b r t", r=2))
                        last.then_inc(cp_out, 1)

                    def low_y(n, kk, src):
                        v_.wait_ge(y_hi, 8 * m + n)
                        v_.tensor_tensor(x_lo[:, kk, :], src, f32(x_hi[:, kk, :]), ALU.subtract).then_inc(y_lo, 1)

                    def out_of_psum(name, dst, bank, n_tiles=2, used=None):
                        if used is not None:
                            v_.wait_ge(unit_used, last_of(ph, used))
                        ins = v_.tensor_tensor(dst, ps[:, bank:bank + n_tiles, 0:T], tok(r_pre, n_tiles, 0), ALU.mult)
                        ins.then_inc(m_evac, 1)

                    ahead(0)
                    ahead(1)
                    pre_rms()
                    v_.wait_ge(unit_used, last_of(ph, 2))
                    v_.tensor_tensor(glow, ps[0:NMETA, 4, 0:T], r_pre[0:NMETA, :], ALU.mult).then_inc(m_evac, 1)
                    v_.wait_ge(m_cleared, m + 1)
                    for r in range(2):
                        rr = slice(r * 64, r * 64 + 64)
                        v_.scalar_tensor_tensor(q[rr, :, r], ps[rr, 0:2, 0:T], 0.125, tok(r_pre, 2, 0)[rr], ALU.mult,
                                                ALU.mult)
                    out_of_psum("qk", k[:, :, :], 2)
                    ahead(2)
                    ahead(3)
                    out_of_psum("v0", v[:, 0:2, :], 6)
                    v_.wait_ge(z_mm, m + 1)
                    for a in range(2):
                        last = v_.tensor_scalar(la[:, a, :], ps[:, a, 0:T], col("gla_b2", layer, a), None, ALU.add)
                    last.then_inc(z_out, 1)
                    out_of_psum("pool", pool_in[:, :, PAD:PAD + T], 2, used=4)
                    v_.wait_ge(lt_step, 3 * m + 3)
                    flat = lambda x_: x_[:, :, :].rearrange("p a t -> p (a t)")
                    c = mark(v_.scalar_tensor_tensor(flat(la), flat(la), 0.0, flat(lt), ALU.min, ALU.subtract))
                    v_.wait_ge(dve, c)
                    c = mark(v_.tensor_scalar(flat(la), flat(la), 1.0 / 16, LOG_DECAY_MIN, ALU.mult, ALU.max))
                    v_.wait_ge(dve, c)
                    for a in range(2):
                        c = mark(v_.tensor_tensor_scan(b[:, a, :], ones[:, 0:T], la[:, a, :], 0.0, ALU.mult, ALU.add))
                    v_.wait_ge(dve, c)
                    exponents(0)
                    exponents(1)
                    out_of_psum("v1", v[:, 2:4, :], 4, used=5)
                    k_decay(0)
                    ahead(4)
                    k_decay(1)
                    ahead(5)
                    exponents(2)
                    out_of_psum("cb", c_b[:, :, :], 0, used=6)
                    exponents(3)
                    v_.wait_ge(masks_in, 16)
                    take_scores(0)
                    k_decay(2)
                    ahead(6)
                    out_of_psum("cc", c_cu[:, 0:2, :], 2, used=7)
                    take_scores(1)
                    k_decay(3)
                    exponents(4)
                    take_scores(2)
                    k_decay(4)
                    exponents(5)
                    exponents(6)
                    ahead(7)
                    out_of_psum("cu", c_cu[:, 2:4, :], 4, used=8)
                    v_.wait_ge(pool_mm, m + 1)
                    for a in range(2):
                        v_.tensor_scalar(y_tmp[:, a, :], ps[:, 6 + a, 0:T], col("pool_scale", layer, a), None, ALU.mult)\
                          .then_inc(y_ready, 1)
                    k_decay(5)
                    k_decay(6)
                    exponents(7)
                    k_decay(7)
                    ahead(8)
                    v_.wait_ge(m_evac, EVACS * m + OUT["cu"])
                    c = mark(v_.tensor_tensor(z_pad[:, :, 2:2 + T], c_cu[:, 0:2, :], c_cu[:, 2:4, :], ALU.mult))
                    v_.wait_ge(dve, c)
                    for a in range(2):
                        c = mark(v_.tensor_scalar(c_cu[:, a, :], z_pad[:, a, 2:2 + T], col("conv_w", layer, 4 + a),
                                                  None, ALU.mult))
                    for j in (1, 0):
                        for a in range(2):
                            v_.wait_ge(dve, c - 1)
                            c = mark(v_.scalar_tensor_tensor(c_cu[:, a, :], z_pad[:, a, j:j + T],
                                                             col("conv_w", layer, 2 * j + a), c_cu[:, a, :],
                                                             ALU.mult, ALU.add))
                    for a in range(2):
                        v_.wait_ge(dve, c - 1 + a)
                        v_.tensor_tensor(c_cu[:, a, :], c_cu[:, a, :], c_b[:, a, :], ALU.mult).then_inc(y_ready, 1)
                    v_.wait_ge(o_sq, m + 1)
                    sq_o = qd[:, 0].rearrange("p a b t -> p (a b t)")
                    v_.tensor_reduce(small[:, 0, 0:8], sq_o[:, 0:1024].rearrange("p (a n) -> p a n", a=8),
                                     mybir.AxisListType.X, ALU.add)
                    c = mark(v_.tensor_reduce(
                        small[0:TAIL, 0, 8:12],
                        kd[0:TAIL].rearrange("p a b t -> p (a b t)")[:, 0:512].rearrange("p (a n) -> p a n", a=4),
                        mybir.AxisListType.X, ALU.add))
                    v_.wait_ge(dve, c)
                    rsqrt(small[:, 0], P, small[:, 1], small[:, 2], small[:, 3])
                    for ch in range(3):
                        n = P if ch < 2 else TAIL
                        last = v_.tensor_tensor(
                            v_tok[0:n, ch, :].rearrange("p (a e) -> p a e", a=4),
                            ps[0:n, 4 + ch, :].rearrange("p (a e) -> p a e", a=4),
                            small[0:n, 3, 4 * ch:4 * ch + 4].unsqueeze(2).to_broadcast([n, 4, P]), ALU.mult)
                    last.then_inc(o_norm, 1)
                    out_of_psum("g0", g_out[:, 0:2, :], 0, used=9)
                    ahead(9)
                    out_of_psum("g1", g_out[:, 2:4, :], 2, used=10)
                    for kk in range(4):
                        low_y(kk + 1, kk, (y_tmp if kk < 2 else c_cu)[:, kk % 2, :])
                    v_.wait_ge(o_tr, m + 1)
                    v_.wait_ge(g_silu, m + 1)
                    for a in range(4):
                        v_.scalar_tensor_tensor(y_head[:, a, :], ps[:, 4 + a, 0:T], col("gla_norm", layer, a),
                                                g_out[:, a, :], ALU.mult, ALU.mult).then_inc(y_ready, 1)
                        if a > 0:
                            low_y(a + 4, 3 + a, y_head[:, a - 1, :])
                    low_y(8, 7, y_head[:, 3, :])
                    ahead(10)
                    ahead(11)
                    ahead(12)
                    sum_squares(1, t_end)
                    ahead(13)
                    sum_squares(2, t_end)
                v_.wait_ge(post_root, bnd + 1)
                c = mark(v_.reciprocal(r_post[:, t_end:T], r_post[:, t_end:T]))
                v_.wait_ge(dve, c)
                final = bnd == NB - 1
                if final:
                    v_.sem_inc(r_out, 1)
                nx = phases[min(bnd + 1, NB - 1)]
                new_h(bnd + 1, POST[ph["kind"]], PRE[nx["kind"]], layer, nx["layer"], t_end, final)
            v_.wait_ge(ends_tr, 2 + KT + 4)
            v_.tensor_copy(out_tok[:, 1, 512:1024], ps[:, 3, :]).then_inc(staged[3], 1)

        @block.gpsimd
        def _(pool):
            pool.memset(wp[:, :, :, :], 0.0).then_inc(zeroed, 1)
            pool.memset(small[:, :, :], 1.0)
            pool.sem_inc(hid_lo_ready, 1)
            pool.sem_inc(hid_lo_ready, 1)
            for ph in phases:
                bnd, t0 = ph["b"], ph["t_in"]
                one = pre_acc[:, 0:1]
                for n, (dst, a0, a1, tiles) in enumerate((
                        (pre_acc, f[:, 0:2], f[:, 2:4], 4), (pre_acc, pre_acc, f[:, 4:6], 6),
                        (one, one, pre_acc[:, 1:2], 6), (one, one, f[:, 6:7], 7), (one, one, f[:, 7:8], 8))):
                    pool.wait_ge(sq_ready, 8 * bnd + tiles)
                    if n:
                        pool.wait_ge(pre_sum, 5 * bnd + n)
                    pool.tensor_tensor(dst[:, :, t0:T], a0[:, :, t0:T], a1[:, :, t0:T], ALU.add).then_inc(pre_sum, 1)
                if ph["kind"] != "mix":
                    fi = ph["f"]

                    def group(parity, idx, dst_hi, dst_lo):
                        pool.wait_ge(silu_done, idx)
                        pool.wait_ge(up_evac, idx + 2)
                        pool.tensor_tensor(up[:, parity, :, t0:T], gate[:, parity, :, t0:T],
                                           up[:, parity, :, t0:T], ALU.mult).then_inc(hid_mul, 1)
                        pool.wait_ge(hid_hi_ready, idx)
                        pool.tensor_tensor(dst_lo, up[:, parity, :, t0:T], f32(dst_hi), ALU.subtract)\
                            .then_inc(hid_lo_ready, 1)

                    group(0, GROUPS * fi + 1, hid_hi[:, 0:2, t0:T], hid_lo[:, 0:2, t0:T])
                    with pool.Fori(0, GROUPS // 2) as i:
                        for g in (1, 2):
                            tiles = bass.ds(i * 4 + 2 * g, 2)
                            group(g % 2, i * 2 + (GROUPS * fi + g + 1), hid_hi[:, tiles, t0:T], hid_lo[:, tiles, t0:T])
                else:
                    m = ph["m"]
                    pool.wait_ge(pre_sum, 5 * bnd + 5)
                    pool.memset(s_diag[:, :, :, :], 0.0)
                    pool.memset(s_last[:, :, :], 0.0)
                    pool.memset(z_pad[:, :, 0:2], 0.0)
                    pool.memset(q[:, :, :, :], 0.0)
                    pool.memset(qd[:, 1], 0.0)
                    pool.memset(kd[:, 1], 0.0)
                    for w in (pool_in, win_a, win_b):
                        last = pool.memset(w[:, :, 0:PAD], 0.0)
                    last.then_inc(m_cleared, 1)
                    pool.wait_ge(m_cleared, m + 1)

                    def q_decay(j):
                        pool.wait_ge(dec_exp, JOBS * m + j + 1)
                        if j >= 2:
                            pool.wait_ge(job_mm, JOBS * m + j - 1)
                        if j == 0:
                            queries = lambda x_: x_[:, :, :]
                        elif j == JOBS - 1:
                            queries = lambda x_: x_[:, :, 2 * P:T]
                        else:
                            bs = 2 * BASE << (j - 1)
                            n = T if T % bs == 0 else 2 * P
                            by = lambda x_: x_[:, :, 0:n].rearrange("p a (n s) -> p a n s", s=bs)
                            queries = lambda x_: by(x_)[:, :, :, bs // 2:bs]
                        for r in range(2):
                            last = pool.tensor_tensor(queries(qd[:, j % 2, :, r]), queries(q[:, :, r]),
                                                      queries(dec[:, j % 2]), ALU.mult)
                        last.then_inc(q_dec, 1)

                    pool.wait_ge(masks_in, 16)
                    pool.wait_ge(m_evac, EVACS * m + OUT["pool"])
                    step = [8 * m]

                    def own(ins):
                        ins.then_inc(pool_own, 1)
                        step[0] += 1
                        pool.wait_ge(pool_own, step[0])
                    now = slice(PAD, PAD + T)
                    back = lambda n: slice(PAD - n, PAD - n + T)
                    lo_, hi_ = slice(0, 64), slice(64, P)
                    own(pool.tensor_tensor(win_a[:, :, now], pool_in[:, :, now], pool_in[:, :, back(1)], ALU.add))
                    own(pool.tensor_tensor(win_b[:, :, now], win_a[:, :, now], win_a[:, :, back(2)], ALU.add))
                    own(pool.tensor_tensor(y_tmp[lo_, 0, :], win_a[lo_, 0, now], inv_count[lo_, 0], ALU.mult))
                    own(pool.tensor_tensor(y_tmp[hi_, 0, :], win_b[hi_, 0, now], inv_count[hi_, 0], ALU.mult))
                    own(pool.tensor_tensor(win_a[:, 1, now], win_b[:, 1, now], win_b[:, 1, back(4)], ALU.add))
                    own(pool.tensor_tensor(y_tmp[lo_, 1, :], win_a[lo_, 1, now], inv_count[lo_, 1], ALU.mult))
                    own(pool.tensor_tensor(win_b[hi_, 1, now], win_a[hi_, 1, now], win_a[hi_, 1, back(8)], ALU.add))
                    own(pool.tensor_tensor(y_tmp[hi_, 1, :], win_b[hi_, 1, now], inv_count[hi_, 1], ALU.mult))
                    pool.tensor_tensor(y_tmp[:, :, :], y_tmp[:, :, :], pool_in[:, :, now], ALU.subtract)\
                        .then_inc(pool_win, 1)
                    assert step[0] == 8 * (m + 1)
                    for j in range(JOBS):
                        q_decay(j)
            pool.wait_ge(r_out, 1)
            pool.wait_ge(pair_out, 4 * NB)
            for kk in range(LATE, KT, 2):
                pool.tensor_tensor(f[:, kk:kk + 2, t0:T], f[:, kk:kk + 2, t0:T],
                                   r_post[:, t0:T].unsqueeze(1).to_broadcast([P, 2, T - t0]), ALU.mult)\
                    .then_inc(late_scaled, 1)

        @block.tensor
        def _(pe):
            def mm3(out_, wh, wl, xh, xl, first, last):
                pe.matmul(out_, wh, xh, start=first, stop=False)
                pe.matmul(out_, wh, xl, start=False, stop=False)
                return pe.matmul(out_, wl, xh, start=False, stop=last)

            def unit(slot, count, view, k_list, m_list, bank, xs, t0, k_first, k_last, high=None, low=None,
                     m_sets=None, after=None, before_last=None, at=-1):
                pe.wait_ge(unit_lo, count)
                xh, xl = xs
                m_sets = m_sets or [m_list]

                def low_part(kk, kg, ms_):
                    pe.wait_ge(*low(kg))
                    for mm in ms_:
                        last = pe.matmul(ps[:, bank + mm, 0:T - t0], view(w_hi, kk, mm), xl[:, kg, t0:T],
                                         start=False, stop=kg == k_last)
                    return last
                for n, ms_ in enumerate(m_sets):
                    for kk, kg in enumerate(k_list):
                        if before_last and n == len(m_sets) - 1 and kk == at % len(k_list):
                            before_last()
                        outs = [ps[:, bank + mm, 0:T - t0] for mm in ms_]
                        if high:
                            pe.wait_ge(*high(kg))
                        for o, mm in zip(outs, ms_):
                            if not high:
                                last = mm3(o, view(w_hi, kk, mm), view(w_lo, kk, mm), xh[:, kg, t0:T], xl[:, kg, t0:T],
                                           kg == k_first, kg == k_last)
                            else:
                                pe.matmul(o, view(w_hi, kk, mm), xh[:, kg, t0:T], start=kg == k_first, stop=False)
                                pe.matmul(o, view(w_lo, kk, mm), xh[:, kg, t0:T], start=False, stop=False)
                        if high and kk:
                            low_part(kk - 1, kg - 1, ms_)
                    if high:
                        last = low_part(kk, kg, ms_)
                    if after and n < len(m_sets) - 1 and after[n] is not None:
                        last.then_inc(after[n], 1)
                last.then_inc(unit_used, 1)

            def up_view(slot):
                def view(w, kk, mm):
                    tiles = w[:, slot].rearrange("p (s k n) -> p s k n", s=2, k=4)
                    return tiles[:, mm // 2, kk, (mm % 2) * P:(mm % 2 + 1) * P]
                return view

            def k_view(slot, nk, n):
                def view(w, kk, mm):
                    return w[:, slot, 0:nk * n].rearrange("p (k n) -> p k n", k=nk)[:, kk, mm * P:(mm + 1) * P]
                return view

            def sum_h(ph, t0):
                pe.wait_ge(pre_sum, 5 * ph["b"] + 5)
                pe.matmul(ps[:, sum_bank(ph), 0:T - t0], ones[:, 0:P], pre_acc[:, 0, t0:T], start=True, stop=True)\
                  .then_inc(ss_pre, 1)

            def sum_f(blk, t0, part):
                if part == 0:
                    pe.wait_ge(sq_sum, 3 * blk + 3)
                else:
                    pe.wait_ge(sq_pair, 5 * blk + 3 + part)
                src = sq_new[:, part - 1, t0:T] if part else sq_acc[:, 0, t0:T]
                ins = pe.matmul(ps[:, 3, 0:T - t0], ones[:, 0:P], src, start=part == 0, stop=part == 2)
                if part == 2:
                    ins.then_inc(ss_post, 1)

            def stay_warm(bank, products):
                for _ in range(products):
                    pe.matmul(ps[:, bank, 0:T], ones[:, 0:P], ones[:, :], start=True, stop=True)

            for _ in range(RING):
                pe.sem_inc(unit_used, 1)
            pe.wait_ge(ones_set, 1)
            stay_warm(0, WARM_START)
            pe.wait_ge(ident_in, 16)
            pe.wait_ge(gain_in, 16)
            pe.transpose(ps[:, 7, T:T + n_first], par_rows[0:n_first, :], ident[0:n_first, 0:n_first])\
              .then_inc(ends_tr, 1)
            pe.wait_ge(x_in, 48)
            for kk in range(KT):
                if kk == KT - 1:
                    pe.wait_ge(par_ready, 1)
                pe.transpose(ps[:, kk, 0:NMETA], meta_tok[:, kk * P:(kk + 1) * P], ident[0:NMETA, 0:NMETA])
                for tt in range(2):
                    last = pe.transpose(ps[:, kk, NMETA + tt * P:NMETA + (tt + 1) * P],
                                        x_tok[:, tt, kk * P:(kk + 1) * P], ident)
                last.then_inc(ends_tr, 1)

            pe.wait_ge(h_ready, 4)
            for ph in phases:
                u0, layer, bnd, t0 = ph["u0"], ph["layer"], ph["b"], ph["t_in"]
                xs = (x_hi, x_lo)
                x_waits = dict(high=lambda kg: (xh_ready, 8 * bnd + kg + 1), low=lambda kg: (xl_ready, 8 * bnd + kg + 1))
                if ph["kind"] != "mix":
                    fi = ph["f"]

                    def group(parity, ja, i4, idx, before_last=None, **waits):
                        pe.wait_ge(up_evac, idx)
                        for j in range(2):
                            u = u0 + ja + j
                            unit(u % RING, i4 + (u + 1 + RING), up_view(u % RING), range(4 * j, 4 * j + 4), range(4),
                                 4 * parity, xs, t0, 0, KT - 1, before_last=before_last if j else None, **waits)

                    def before_last():
                        if bnd == 0:
                            pe.wait_ge(par_in, 16 * (len(rows) - 1))
                            pe.wait_ge(h_ready, KT)
                            pe.transpose(ps[:, 6, T:T + n_rows], par_rows[0:n_rows, :], ident[0:n_rows, 0:n_rows])\
                              .then_inc(ends_tr, 1)
                        sum_h(ph, t0)
                    group(0, 0, 0, GROUPS * fi + 1, before_last=before_last, **x_waits)
                    pe.wait_ge(pre_root, bnd + 1)
                    if bnd == 0:
                        pe.wait_ge(par_ready, 2)
                    with pe.Fori(0, GROUPS // 2) as i:
                        for g in (1, 2):
                            group(g % 2, 2 * g, i * 4, i * 2 + (GROUPS * fi + g + 1))
                    d0 = u0 + UP_UNITS
                    hid = (hid_hi, hid_lo)
                    pe.wait_ge(up_evac, GROUPS * fi + GROUPS + 1)

                    def hid_tile(kg):
                        return (hid_lo_ready, GROUPS * fi + kg // 2 + 1 + 2)
                    for pair in range(KT // 2):
                        if pair >= 2:
                            pe.wait_ge(pair_out, 4 * bnd + pair - 1)
                        k0 = 0
                        for j, nk in enumerate(DOWN_K):
                            u = d0 + 4 * pair + j
                            kw = {}
                            if pair == 0:
                                kw = dict(high=hid_tile, low=hid_tile)
                            if pair == 3 and j == 3:
                                sum_f(bnd, t0, 0)
                                kw = dict(m_sets=[[0], [1]], after=[tile_done], before_last=lambda: sum_f(bnd, t0, 1))
                            unit(u % RING, u + 1 + RING, k_view(u % RING, nk, 256), range(k0, k0 + nk), range(2),
                                 4 + 2 * (pair % 2), hid, t0, 0, FT - 1, **kw)
                            k0 += nk
                    sum_f(bnd, t0, 2)
                else:
                    m, t1 = ph["m"], ph["t_out"]

                    def proj(name, bank, **kw):
                        j = 2 + [n_ for n_, _, _ in PROJ].index(name)
                        n = PROJ[j - 2][2]
                        u = u0 + j
                        unit(u % RING, u + 1 + RING, k_view(u % RING, 8, n), range(8), range(n // P), bank, xs,
                             0, 0, KT - 1, **kw)

                    def wait_out(name):
                        pe.wait_ge(m_evac, EVACS * m + OUT[name])

                    for jj in range(2):
                        u = u0 + jj
                        unit(u % RING, u + 1 + RING, k_view(u % RING, 4, 512), range(4 * jj, 4 * jj + 4), range(4),
                             0, xs, 0, 0, KT - 1, **x_waits)
                    proj("glow", 4)
                    sum_h(ph, 0)
                    proj("v0", 6)
                    wait_out("qk")
                    pe.wait_ge(mix_in, 48)
                    for a in range(2):
                        last = pe.matmul(ps[:, a, 0:T], w2[:, layer, a * P:(a + 1) * P], glow, start=True, stop=True)
                    last.then_inc(z_mm, 1)
                    proj("pool", 2)
                    pe.wait_ge(pre_root, bnd + 1)
                    proj("v1", 4)
                    pe.wait_ge(z_out, m + 1)

                    def v_token_major():
                        wait_out("v1")
                        for hh in range(HEADS):
                            for ch in range(2):
                                pe.transpose(ps[:, 4 + ch, hh * P:(hh + 1) * P], v[:, hh, ch * P:(ch + 1) * P], ident)
                            last = pe.matmul(ps[0:TAIL, 6, hh * P:(hh + 1) * P], v[:, hh, 2 * P:T], ident,
                                             start=True, stop=True)
                        last.then_inc(vt_mm, 1)
                    proj("cb", 0, before_last=v_token_major, at=4)

                    def job(j):
                        bank = JOB_BANK[j]
                        pe.wait_ge(q_dec, JOBS * m + j + 1)
                        pe.wait_ge(k_dec, JOBS * m + j + 1)

                        def score(out_, a, s, t):
                            return pe.matmul(out_, kd[:, j % 2, a, s], qd[:, j % 2, a, :, t], start=True, stop=True)
                        for a in range(2):
                            for ch in range(2):
                                o, at = ch * P, bank + 2 * ch + a
                                if j < MASKED:
                                    last = score(ps[:, at, 0:2 * P], a, slice(o, o + P), slice(o, o + P))
                                elif j < JOBS - 2:
                                    bs = 2 * BASE << (j - 1)
                                    hf = bs // 2
                                    for s0 in range(0, P, bs):
                                        mid_ = o + s0 + hf
                                        last = score(ps[s0:s0 + hf, at, 0:bs], a, slice(mid_ - hf, mid_),
                                                     slice(mid_, mid_ + hf))
                                elif j == JOBS - 2 and ch == 0:
                                    last = score(ps[:, bank + a, 0:2 * P], a, slice(0, P), slice(P, 2 * P))
                                elif j == JOBS - 1:
                                    last = score(ps[:, bank + ch, 2 * a * TAIL:2 * (a + 1) * TAIL], a,
                                                 slice(o, o + P), slice(2 * P, T))
                            if j < MASKED:
                                last = score(ps[0:TAIL, bank + a, 2 * P:2 * P + 2 * TAIL], a,
                                             slice(2 * P, T), slice(2 * P, T))
                        last.then_inc(job_mm, 1)

                    def taken(n):
                        pe.wait_ge(cp_out, MASKED * m + n)

                    def act_has(n):
                        pe.wait_ge(act_out, 6 * m + n)

                    act_has(1)
                    job(0)
                    wait_out("pool")
                    proj("cc", 2)
                    taken(1)
                    job(1)
                    wait_out("cc")
                    job(2)
                    taken(2)
                    proj("cu", 4)
                    taken(3)
                    job(3)
                    pe.wait_ge(pool_win, m + 1)
                    for a in range(2):
                        last = pe.matmul(ps[:, 6 + a, 0:T], wp[:, layer, a, :], y_tmp[:, a, :], start=True, stop=True)
                    last.then_inc(pool_mm, 1)
                    act_has(2)
                    job(4)
                    wait_out("cu")
                    pe.wait_ge(y_ready, 8 * m + 2)
                    job(5)
                    act_has(3)
                    job(6)
                    act_has(4)
                    job(7)
                    act_has(6)
                    pe.wait_ge(act_out, 4 * m + 4)
                    for ch in range(3):
                        for hh in range(HEADS):
                            n = P if ch < 2 else TAIL
                            parts = [(s_diag[:, 0, hh], 0)] if ch == 0 else \
                                [(s_next[:, hh, 0:P], 0), (s_diag[:, 1, hh], 1)] if ch == 1 else \
                                [(s_next[:, hh, P:P + TAIL], 0), (s_tail[:, hh], 1), (s_last[:, hh], 2)]
                            for n_, (sc, cs) in enumerate(parts):
                                vv = v_tok[:, cs] if cs < 2 else v_tok[0:TAIL, cs]
                                last = pe.matmul(ps[0:n, 4 + ch, hh * P:(hh + 1) * P], sc, vv[:, hh * P:(hh + 1) * P],
                                                 start=n_ == 0, stop=n_ == len(parts) - 1)
                    last.then_inc(o_mm, 1)

                    def out_unit(j, bank, **kw):
                        u = u0 + j
                        kh = 4 * ((j - 11) % 2)
                        unit(u % RING, u + 1 + RING, k_view(u % RING, 4, 512), range(kh, kh + 4), range(4),
                             bank, xs, t1, 0, KT - 1, **kw)
                    proj("g0", 0)
                    proj("g1", 2)
                    pe.wait_ge(o_norm, m + 1)
                    for hh in range(HEADS):
                        for ch in range(2):
                            pe.transpose(ps[:, 4 + hh, ch * P:(ch + 1) * P], v_tok[:, ch, hh * P:(hh + 1) * P], ident)
                        last = pe.transpose(ps[:, 4 + hh, 2 * P:T], v_tok[0:TAIL, 2, hh * P:(hh + 1) * P],
                                            ident[0:TAIL, 0:TAIL])
                    last.then_inc(o_tr, 1)
                    wait_out("g1")
                    y_waits = dict(high=lambda kg: (y_hi, 8 * m + kg + 1), low=lambda kg: (y_lo, 8 * m + kg + 1))
                    out_unit(11, 0, **y_waits)
                    out_unit(12, 0, **y_waits)
                    out_unit(13, 4)
                    out_unit(14, 4, m_sets=[[0, 1], [2], [3]], after=[half_done, tile_done],
                             before_last=lambda: (sum_f(bnd, t1, 0), sum_f(bnd, t1, 1)))
                    sum_f(bnd, t1, 2)
                pe.wait_ge(post_root, bnd + 1)
                stay_warm(3, WARM_BOUNDARY)
            for half in range(2):
                for tt in range(2):
                    for kk in range(4 * half, 4 * half + 4):
                        pe.wait_ge(h_ready, 8 * NB + kk + 1)
                        last = pe.transpose(ps[:, 2 * tt + half, (kk % 4) * P:(kk % 4 + 1) * P],
                                            h[:, kk, NMETA + tt * P:NMETA + (tt + 1) * P], ident)
                    last.then_inc(ends_tr, 1)


_INS = ["x", "meta", "ffn1_pre", "ffn1_post", "ffn1_wg", "ffn1_wu", "ffn1_wd", "mix_pre", "mix_post", "w_in",
        "pool_w", "pool_scale", "conv_w", "gla_w2", "gla_b2", "gla_norm", "w_out",
        "ffn2_pre", "ffn2_post", "ffn2_wg", "ffn2_wu", "ffn2_wd"]


def kernel(**inputs):
    import concourse.bacc as bacc
    from concourse.bass_utils import run_bass_kernel_spmd

    nc = bacc.Bacc("TRN2", target_bir_lowering=False, num_devices=1)
    arrays = {f"in_{n}": np.ascontiguousarray(inputs[n]) for n in _INS}
    arrays["in_consts"] = shape_constants(inputs["x"].shape[1] + NMETA)
    args = [nc.dram_tensor(n, a.shape, mybir.dt.from_np(a.dtype), kind="ExternalInput").ap()
            for n, a in arrays.items()]
    out = nc.dram_tensor("out", inputs["x"].shape, F32, kind="ExternalOutput").ap()
    trunk(nc, *args, out)
    r = run_bass_kernel_spmd(nc, [arrays], core_ids=[0])
    return r.results[0]["out"]
```
